# Optimizing a Trainium2 kernel written in Bass

```python
import jax, jax.numpy as jnp
from jax import lax
import numpy as np

D_MODEL = 1024
BATCH = 1
SEQ = 256
DEPTH = 2

N_META = 16
CHUNK = 128
RET_HEADS = 8
RET_DK = D_MODEL // (2 * RET_HEADS)
RET_DV = 2 * RET_DK
SB_HEADS = 8
SB_DH = D_MODEL // (2 * SB_HEADS)
D_FF = ((8 * D_MODEL // 3 + 255) // 256) * 256
ROPE_BASE = 10000.0
EPS = 1e-6

COL_SIZES = [RET_HEADS * RET_DK, RET_HEADS * RET_DK, RET_HEADS * RET_DV, RET_HEADS * RET_DV,
             SB_HEADS * SB_DH, SB_HEADS * SB_DH, SB_HEADS * SB_DH, D_MODEL, D_MODEL]
D_IN = int(sum(COL_SIZES))
SPLITS = [int(s) for s in np.cumsum(COL_SIZES)[:-1]]

kernel_name = "hybrid_retention_stickbreaking_macaron"

def rmsnorm(x, g):
    xf = x.astype(jnp.float32)
    r = lax.rsqrt(jnp.mean(xf * xf, axis=-1, keepdims=True) + EPS)
    return (xf * r).astype(x.dtype) * g

def swiglu(x, w_gu, w_down):
    a, b = jnp.split(x @ w_gu, 2, axis=-1)
    return (jax.nn.silu(a) * b) @ w_down

def rotary(t, pos):
    dh = t.shape[-1]
    freqs = ROPE_BASE ** (-jnp.arange(0, dh, 2, dtype=jnp.float32) / dh)
    ang = pos[:, None] * freqs[None, :]
    cos, sin = jnp.cos(ang), jnp.sin(ang)
    tf = t.astype(jnp.float32)
    t1, t2 = tf[..., : dh // 2], tf[..., dh // 2:]
    return jnp.concatenate([t1 * cos - t2 * sin, t1 * sin + t2 * cos], axis=-1).astype(t.dtype)

def retention(q, k, v, valid):
    B, H, L, dk = q.shape
    dv = v.shape[-1]
    N = L // CHUNK
    log_gamma = jnp.log(1.0 - 2.0 ** (-5.0 - jnp.arange(H, dtype=jnp.float32)))
    vmask = valid.astype(jnp.float32)[None, None, :, None]
    qf = q.astype(jnp.float32).reshape(B, H, N, CHUNK, dk)
    kf = (k.astype(jnp.float32) * vmask * dk ** -0.5).reshape(B, H, N, CHUNK, dk)
    vf = (v.astype(jnp.float32) * vmask).reshape(B, H, N, CHUNK, dv)
    idx = jnp.arange(CHUNK, dtype=jnp.float32)
    diff = idx[:, None] - idx[None, :]
    decay = jnp.where(diff >= 0, jnp.exp(log_gamma[:, None, None] * jnp.maximum(diff, 0.0)), 0.0)
    scores = jnp.einsum('bhncd,bhnsd->bhncs', qf, kf) * decay[None, :, None]
    o_intra = jnp.einsum('bhncs,bhnse->bhnce', scores, vf)
    k_decay = jnp.exp(log_gamma[:, None] * (CHUNK - 1 - idx)[None, :])
    kv = jnp.einsum('bhnsd,bhnse->bhnde', kf * k_decay[None, :, None, :, None], vf)
    chunk_decay = jnp.exp(log_gamma * CHUNK)[None, :, None, None]

    def step(R, kv_n):
        return R * chunk_decay + kv_n, R

    _, R_prev = lax.scan(step, jnp.zeros((B, H, dk, dv), jnp.float32), jnp.moveaxis(kv, 2, 0))
    R_prev = jnp.moveaxis(R_prev, 0, 2)
    q_decay = jnp.exp(log_gamma[:, None] * (idx + 1.0)[None, :])
    o_cross = jnp.einsum('bhncd,bhnde->bhnce', qf, R_prev) * q_decay[None, :, None, :, None]
    return (o_intra + o_cross).reshape(B, H, L, dv)

def stick_breaking(q, k, v, valid):
    B, H, L, dh = q.shape
    NB = L // CHUNK
    kf = k.astype(jnp.float32)
    vf = v.astype(jnp.float32)
    qb = jnp.moveaxis(q.astype(jnp.float32).reshape(B, H, NB, CHUNK, dh), 2, 0)
    kpos = jnp.arange(L)
    scale = dh ** -0.5

    def block(args):
        q_blk, n = args
        qpos = n * CHUNK + jnp.arange(CHUNK)
        z = jnp.einsum('bhqd,bhkd->bhqk', q_blk, kf) * scale
        mask = ((kpos[None, :] < qpos[:, None]) & valid[None, :])[None, None]
        log_1mb = jnp.where(mask, jax.nn.log_sigmoid(-z), 0.0)
        acc = lax.cumsum(log_1mb, axis=3, reverse=True) - log_1mb
        a = jnp.where(mask, jnp.exp(jax.nn.log_sigmoid(z) + acc), 0.0)
        return jnp.einsum('bhqk,bhkd->bhqd', a, vf)

    o = lax.map(block, (qb, jnp.arange(NB)))
    return jnp.moveaxis(o, 0, 2).reshape(B, H, L, dh)

def mixer(u, w_in, ret_gn, w_ret_proj, w_sb_proj, w_out, pos, valid):
    B, L, _ = u.shape
    rq, rk, rv, rg, sq, sk, sv, ga, gb = jnp.split(u @ w_in, SPLITS, axis=-1)

    def heads(t, n):
        return t.reshape(B, L, n, -1).transpose(0, 2, 1, 3)

    o_r = retention(rotary(heads(rq, RET_HEADS), pos), rotary(heads(rk, RET_HEADS), pos),
                    heads(rv, RET_HEADS), valid)
    mu = jnp.mean(o_r, axis=-1, keepdims=True)
    var = jnp.mean(jnp.square(o_r - mu), axis=-1, keepdims=True)
    o_r = ((o_r - mu) * lax.rsqrt(var + EPS)).transpose(0, 2, 1, 3).reshape(B, L, RET_HEADS * RET_DV)
    y_ret = (jax.nn.silu(rg) * (o_r.astype(u.dtype) * ret_gn)) @ w_ret_proj
    o_s = stick_breaking(heads(sq, SB_HEADS), heads(sk, SB_HEADS), heads(sv, SB_HEADS), valid)
    y_sb = o_s.transpose(0, 2, 1, 3).reshape(B, L, SB_HEADS * SB_DH).astype(u.dtype) @ w_sb_proj
    return (jax.nn.sigmoid(ga) * y_ret + jax.nn.sigmoid(gb) * y_sb) @ w_out

def setup_inputs(seed: int = 0) -> dict:
    key = jax.random.key(seed)
    ks = jax.random.split(key, 20)
    f32 = jnp.float32

    def w(k, shape, fan_in):
        return jax.random.normal(k, shape, f32) * fan_in ** -0.5

    def gain(k, shape):
        return 1.0 + 0.01 * jax.random.normal(k, shape, f32)

    return {
        "x": jax.random.normal(ks[0], (BATCH, SEQ, D_MODEL), f32),
        "meta": jax.random.normal(ks[1], (N_META, D_MODEL), f32),
        "ffn1_norm": gain(ks[2], (DEPTH, D_MODEL)),
        "ffn1_w_gu": w(ks[3], (DEPTH, D_MODEL, 2 * D_FF), D_MODEL),
        "ffn1_w_down": w(ks[4], (DEPTH, D_FF, D_MODEL), D_FF),
        "mix_norm": gain(ks[5], (DEPTH, D_MODEL)),
        "w_in": w(ks[6], (DEPTH, D_MODEL, D_IN), D_MODEL),
        "ret_gn": gain(ks[7], (DEPTH, RET_HEADS * RET_DV)),
        "w_ret_proj": w(ks[8], (DEPTH, RET_HEADS * RET_DV, D_MODEL), RET_HEADS * RET_DV),
        "w_sb_proj": w(ks[9], (DEPTH, SB_HEADS * SB_DH, D_MODEL), SB_HEADS * SB_DH),
        "w_out": w(ks[10], (DEPTH, D_MODEL, D_MODEL), D_MODEL),
        "ffn2_norm": gain(ks[11], (DEPTH, D_MODEL)),
        "ffn2_w_gu": w(ks[12], (DEPTH, D_MODEL, 2 * D_FF), D_MODEL),
        "ffn2_w_down": w(ks[13], (DEPTH, D_FF, D_MODEL), D_FF),
        "final_norm": gain(ks[14], (D_MODEL,)),
    }

def reference(x, meta, ffn1_norm, ffn1_w_gu, ffn1_w_down, mix_norm, w_in, ret_gn,
              w_ret_proj, w_sb_proj, w_out, ffn2_norm, ffn2_w_gu, ffn2_w_down, final_norm):
    B, S, D = x.shape
    pad = CHUNK - N_META
    h = jnp.concatenate([jnp.zeros((B, pad, D), x.dtype),
                         jnp.broadcast_to(meta.astype(x.dtype)[None], (B, N_META, D)), x], axis=1)
    L = S + CHUNK
    idx = jnp.arange(L)
    valid = idx >= pad
    pos = (idx - pad).astype(jnp.float32)
    for l in range(DEPTH):
        h = h + 0.5 * swiglu(rmsnorm(h, ffn1_norm[l]), ffn1_w_gu[l], ffn1_w_down[l])
        h = h + mixer(rmsnorm(h, mix_norm[l]), w_in[l], ret_gn[l], w_ret_proj[l],
                      w_sb_proj[l], w_out[l], pos, valid)
        h = h + 0.5 * swiglu(rmsnorm(h, ffn2_norm[l]), ffn2_w_gu[l], ffn2_w_down[l])
    h = rmsnorm(h, final_norm)
    return h[:, CHUNK:]


_drawn_inputs = setup_inputs


def setup_inputs(seed=0):
    import zlib

    import numpy as np

    out = dict(_drawn_inputs(seed))
    spreads = {}
    factors = {'ffn1_norm': 7.91, 'mix_norm': 5.114, 'ret_gn': 8.0, 'ffn2_norm': 8.0, 'final_norm': 5.756}
    for name, (base, spread) in spreads.items():
        noise = np.random.default_rng([zlib.crc32(name.encode()), seed]).standard_normal(out[name].shape)
        drawn = base * np.exp(spread * noise) if base else spread * noise
        out[name] = __import__('jax').numpy.asarray(drawn.astype(out[name].dtype))
    for name, factor in factors.items():
        out[name] = (out[name] * factor).astype(out[name].dtype)
    return out
```

```python
from contextlib import ExitStack

import concourse.bass as bass
import numpy as np
from concourse import mybir

F32 = mybir.dt.float32
F32R = mybir.dt.float32r
ALU = mybir.AluOpType
ACT = mybir.ActivationFunctionType

P = 128
D = 1024
DEPTH = 2
N_META = 16
SEQ = 256
T = N_META + SEQ
HEADS = 8
DK = 64
DV = 128
D_FF = 2816
EPS = 1e-6
DC = D // P
FC = D_FF // P
ITERS = FC // 2
BLOCKS = 8
PIECE = BLOCKS * P
RING = 4
TOK = [(0, P), (P, P), (2 * P, T - 2 * P)]
SEG = [0, T, T + (T - P)]
SCORES = T + (T - P) + (T - 2 * P)
PADT = 3 * P

GU = 4 * ITERS
QUADS = 2
FFN = GU + QUADS * ITERS
U_Q, U_K, U_V, U_G, U_SQ, U_SK, U_SV, U_GA, U_GB, U_Y = 0, 2, 4, 8, 12, 14, 16, 18, 22, 26
Y_UNITS = [("r", 0), ("r", 1), ("s", 0), ("s", 1), ("r", 2), ("s", 2), ("r", 3), ("s", 3)]
Y_STEPS = [(j, kind, pr, half) for j, (kind, pr) in enumerate(Y_UNITS) for half in range(2 if kind == "r" else 1)]
Y_BANKS = [0, 2, 4]
S_Y = 2 * U_Y
S_OUT = S_Y + len(Y_STEPS)
MIX = S_OUT + 8
OUT_BANKS = [6, 4, 0, 2]
OUT_AFTER = [None, 5, 6, 7]
PER_LAYER = 2 * FFN + MIX
UNITS = U_Y + len(Y_UNITS)
PAIRS = DC // 2
ADDS = PAIRS - 1
RET0, SB0 = 2 * U_SQ, 37
NEG = -2.0 ** 100

C_COS, C_SIN, C_DECAY = 0, T, 2 * T
C_ONES, C_IDENT, C_CENTRE, C_NEG, C_CUM, C_ALL = (P * i for i in range(6))


def trunk(nc, stream, h_in, gains, gn_gains, tables, squares, h_out):
    with ExitStack() as ctx:
        def sb(name, shape, dt=F32):
            return ctx.enter_context(nc.sbuf_tensor(name, shape, dt))

        def sem(name):
            return ctx.enter_context(nc.semaphore(name))

        raw = sb("raw", [P, RING, PIECE])
        w_hi = sb("w_hi", [P, RING, PIECE], F32R)
        w_lo = sb("w_lo", [P, RING, PIECE], F32R)
        h = sb("h", [P, DC, T])
        xh = sb("xh", [P, DC, T], F32R)
        xl = sb("xl", [P, DC, T], F32R)
        gh = sb("gh", [P, FC, T], F32R)
        gl = sb("gl", [P, FC, T], F32R)
        RET_C, SB_C, MERGE_C = 0, 8, 12
        rq = sb("rq", [P, 4, T])
        rk = sb("rk", [P, 4, PADT])
        rv = sb("rv", [P, 3, D])
        rg = sb("rg", [P, DC, T])
        sq = sb("sq", [P, 4, T])
        sk = sb("sk", [P, 4, PADT])
        sv = sb("sv", [P, 3, D // 2])
        ga = rg
        gb = rv[:, :, :].rearrange("p a b -> p (a b)")[:, 0:DC * T].rearrange("p (c t) -> p c t", t=T)
        table = sb("table", [P, C_DECAY + HEADS * SCORES])
        square = sb("square", [P, 6 * P])
        neg_r = sb("neg_r", [P, P], F32R)
        ident_r = sb("ident_r", [P, P], F32R)
        gain = sb("gain", [P, 3 * DEPTH + 1, DC])
        gn_gain = sb("gn_gain", [P, DEPTH, HEADS])
        eps = sb("eps", [P, 1])
        scl = sb("scl", [P, 2, T])
        act = sb("act", [P, 2, T])
        gv = sb("gv", [P, 2, T])
        xg = sb("xg", [P, 2, 2, T])
        sqh = sb("sqh", [P, 2, T])
        ssq = sb("ssq", [P, 2, T])
        ms = sb("ms", [P, T])
        r = sb("r", [P, T])
        dec = sb("dec", [P, SCORES])
        ro = sb("ro", [P, T])
        rs, rr = gv[:, 0, :], gv[:, 1, :]
        rn = xg[:, 1, 0, :]
        sa = ssq[:, :, :].rearrange("p a t -> p (a t)")[:, 0:SCORES]
        sp = sqh[:, :, :].rearrange("p a t -> p (a t)")[:, 0:SCORES]
        pa = xg[:, 0, :, :].rearrange("p a t -> p (a t)")[:, 0:SCORES]
        bank = ctx.enter_context(nc.psum_tensor("bank", [P, 8, 512], F32))

        cos, sin = table[:, C_COS:C_COS + T], table[:, C_SIN:C_SIN + T]
        ones, ident, centre, neg, cum, allneg = (square[:, c:c + P] for c in (C_ONES, C_IDENT, C_CENTRE, C_NEG, C_CUM, C_ALL))

        bank67 = bank[:, 6:8, :].rearrange("p b c -> p (b c)")

        def strided_pair(c, step, n):
            return bank67[:, c:c + 2 * step].rearrange("p (i q) -> p i q", i=2)[:, :, 0:n]

        def twice(ap, q0):
            return ap[:, q0:T].unsqueeze(1).to_broadcast([P, 2, T - q0])

        def pair(n, q0):
            return bank[:, n:n + 2, q0:T]

        def first_query(l):
            return N_META if isinstance(l, int) and l == DEPTH - 1 else 0

        def layers(eng, layer):
            with eng.Fori(0, DEPTH - 1) as l:
                layer(l)
            layer(DEPTH - 1)

        raw_ready = [sem(f"raw_ready{i}") for i in range(RING)]
        hi_ready, lo_ready, piece_done = sem("hi_ready"), sem("lo_ready"), sem("piece_done")
        gains_in, gn_gains_in, table_in, squares_in = sem("gains_in"), sem("gn_gains_in"), sem("table_in"), sem("squares_in")
        h_loaded = [sem(f"h_loaded{p}") for p in range(PAIRS)]
        pads_ready, masks_ready, out_stored = sem("pads_ready"), sem("masks_ready"), sem("out_stored")
        scaled_out, out_ready, last_out = sem("scaled_out"), sem("out_ready"), sem("last_out")
        h_new, x_scaled, xh_ready, x_ready = sem("h_new"), sem("x_scaled"), sem("xh_ready"), sem("x_ready")
        sq_ready, ssq_added, ssum_done = sem("sq_ready"), sem("ssq_added"), sem("ssum_done")
        ms_ready, rms_ready, r_ready = sem("ms_ready"), sem("rms_ready"), sem("r_ready")
        gate_scaled, gate_act, up_gated = sem("gate_scaled"), sem("gate_act"), sem("up_gated")
        g_val, gh_ready, g_ready = sem("g_val"), sem("gh_ready"), sem("g_ready")
        unit_evicted, swapped, rot_cos, rot_sin, rotated = sem("unit_evicted"), sem("swapped"), sem("rot_cos"), sem("rot_sin"), sem("rotated")
        v_turned, v_ready, rg_ready, sig_ready = sem("v_turned"), sem("v_ready"), sem("rg_ready"), sem("sig_ready")
        ret_scores, ret_decayed, ret_o, ro_ready = sem("ret_scores"), sem("ret_decayed"), sem("ret_o"), sem("ro_ready")
        rs_ready, ret_var = sem("rs_ready"), sem("ret_var")
        ln_ready, rr_ready, rn_ready, gated, rh_ready, ret_ready = (sem("ln_ready"), sem("rr_ready"), sem("rn_ready"),
                                                                  sem("gated"), sem("rh_ready"), sem("ret_ready"))
        z_done, sa_step, sp_ready, cum_done, pa_ready = sem("z_done"), sem("sa_step"), sem("sp_ready"), sem("cum_done"), sem("pa_ready")
        sbo_done, sbh_ready, sb_ready = sem("sbo_done"), sem("sbh_ready"), sem("sb_ready")
        y_merged, y_b, yh_ready, y_ready = sem("y_merged"), sem("y_b"), sem("yh_ready"), sem("y_ready")

        block = ctx.enter_context(nc.Block())

        @block.sync
        def _(sp_):
            def load(j, n):
                sp_.dma_start(raw[:, j, :], stream[n]).then_inc(raw_ready[j], 16)

            for j in range(RING):
                load(j, j)
            sp_.dma_start(square[:, :], squares).then_inc(squares_in, 16)
            for j in range(RING):
                sp_.wait_ge(lo_ready, j + 1)
                load(j, RING + j)
            sp_.dma_start(table[:, :], tables).then_inc(table_in, 16)
            with sp_.Fori(2, DEPTH * PER_LAYER // RING) as i:
                for j in range(RING):
                    sp_.wait_ge(lo_ready, i * RING + (j - RING + 1))
                    load(j, i * RING + j)
            for p in (0, 1, 3, 2):
                if p < PAIRS - 1:
                    sp_.wait_ge(out_ready, p + 1)
                else:
                    sp_.wait_ge(last_out, 1)
                sp_.dma_start(h_out[:, 2 * p:2 * p + 2, :], h[:, 2 * p:2 * p + 2, N_META:T]).then_inc(out_stored, 16)
            sp_.wait_ge(out_stored, 16 * PAIRS)

        @block.gpsimd
        def _(pool):
            pool.memset(rk[:, :, T:PADT], 0.0).then_inc(pads_ready, 1)
            pool.memset(sk[:, :, T:PADT], 0.0).then_inc(pads_ready, 1)
            pool.memset(eps[:, :], EPS).then_inc(pads_ready, 1)

            def add_squares(rnd, p):
                pool.wait_ge(sq_ready, rnd * PAIRS + (p + 1))
                if p > 1:
                    pool.wait_ge(ssq_added, rnd * ADDS + (p - 1))
                pool.tensor_tensor(ssq[:, :, :], ssq[:, :, :], sqh[:, :, :], ALU.add).then_inc(ssq_added, 1)

            with pool.Fori(0, 3 * DEPTH) as rnd:
                for p in range(1, PAIRS):
                    add_squares(rnd, p)
            for p in range(1, PAIRS - 1):
                add_squares(3 * DEPTH, p)
            pool.wait_ge(r_ready, 3 * DEPTH + 1)
            pool.wait_ge(scaled_out, DC)
            pool.tensor_tensor(h[:, DC - 2:DC, N_META:T], h[:, DC - 2:DC, N_META:T], twice(r, N_META),
                               ALU.mult).then_inc(last_out, 1)

        @block.scalar
        def _(eng):
            def raw_count(n, slot):
                return (n - slot) * (16 // RING) + 16

            def split_hi(n, slot, first=False):
                if not first:
                    eng.wait_ge(piece_done, n - (RING - 1))
                eng.wait_ge(raw_ready[slot], raw_count(n, slot))
                eng.activation(w_hi[:, slot, :], raw[:, slot, :], ACT.Copy).then_inc(hi_ready, 1)

            def hi_of_h(rnd, p, q0, loaded=False, final=False):
                c = 2 * p
                if loaded:
                    eng.wait_ge(h_loaded[p], 16)
                else:
                    eng.wait_ge(h_new, (rnd - 1) * PAIRS + (p + 1))
                if not final:
                    eng.wait_ge(x_scaled, rnd * DC + (c + 2))
                    eng.activation(xh[:, c:c + 2, q0:T], xg[:, p % 2, :, q0:T], ACT.Copy).then_inc(xh_ready, 1)
                if p == 0:
                    eng.activation(ssq[:, :, q0:T], h[:, 0:2, q0:T], ACT.Square).then_inc(sq_ready, 1)
                else:
                    if p > 1:
                        eng.wait_ge(ssq_added, rnd * ADDS + (p - 1))
                    eng.activation(sqh[:, :, q0:T], h[:, c:c + 2, q0:T], ACT.Square).then_inc(sq_ready, 1)

            def rms(rnd, q0):
                eng.wait_ge(ms_ready, rnd + 1)
                eng.activation(r[:, q0:T], ms[:, q0:T], ACT.Sqrt).then_inc(rms_ready, 1)

            def ffn(l, f):
                fi = l * 2 + f
                off = 0 if f == 0 else FFN + MIX
                base = l * PER_LAYER + off
                last = first_query(l) > 0 and f == 1
                q0 = first_query(l) if f else 0
                rms(l * 3 + 2 * f, q0)
                eng.preload_act_table_set("silu_and_others")
                with eng.Fori(0, ITERS) as it:
                    for j in range(4):
                        split_hi(base + it * 4 + (j + RING), (off + j) % RING)
                        if j == 1:
                            eng.wait_ge(gate_scaled, fi * ITERS + it + 1)
                            eng.activation(act[:, :, q0:T], scl[:, :, q0:T], ACT.Silu).then_inc(gate_act, 1)
                    eng.wait_ge(g_val, fi * ITERS + it + 1)
                    eng.activation(gh[:, bass.ds(it * 2, 2), q0:T], gv[:, :, q0:T], ACT.Copy).then_inc(gh_ready, 1)
                eng.preload_act_table_set("sqrt_and_others")
                for q in range(QUADS):
                    for c in range(ITERS):
                        s = GU + q * ITERS + c
                        if c >= ITERS - 2:
                            hi_of_h(l * 3 + 2 * f + 1, 2 * q + c - (ITERS - 2), q0, final=last)
                        if not last or s + RING < FFN:
                            split_hi(base + (s + RING), (off + s) % RING)

            def mixer(l):
                base = l * PER_LAYER + FFN
                qf = first_query(l)
                rms(l * 3 + 1, 0)
                eng.preload_act_table_set("silu_and_others")
                for s in range(MIX):
                    if s >= S_OUT and s % 2:
                        hi_of_h(l * 3 + 2, (s - S_OUT) // 2, qf)
                    split_hi(base + (s + RING), (FFN + s) % RING)
                    u = s // 2
                    if s % 2 and u < U_V:
                        eng.wait_ge(unit_evicted, l * UNITS + (u + 1))
                        for q in range(4):
                            a, b = 32 * q, 32 * (q ^ 1)
                            eng.activation(act[b:b + 32, :, :], scl[a:a + 32, :, :], ACT.Copy).then_inc(swapped, 1)
                    for u0, n, first, dst in ((U_V, 4, 0, rv), (U_SV, 2, 4, sv)):
                        k = s // 2 - 1 - u0
                        if s % 2 == 0 and 0 <= k < n:
                            eng.wait_ge(v_turned, l * 6 + (first + k + 1))
                            b = 4 if u0 == U_V else 6
                            eng.activation(dst[:, 0:2, 256 * k:256 * k + 256],
                                           bank[:, b, :].rearrange("p (i f) -> p i f", i=2), ACT.Copy).then_inc(v_ready, 1)
                            eng.activation(dst[0:TOK[2][1], 2, 256 * k:256 * k + 256],
                                           bank[0:TOK[2][1], b + 1, 0:256], ACT.Copy).then_inc(v_ready, 1)
                    if s % 2 and U_G <= u < U_SQ:
                        eng.wait_ge(unit_evicted, l * UNITS + (u + 1))
                        c = 2 * (u - U_G)
                        eng.activation(rg[:, c:c + 2, qf:T], scl[:, :, qf:T], ACT.Silu).then_inc(rg_ready, 1)
                    if s == RET0:
                        eng.preload_act_table_set("natural_log_exp_and_others")
                    hd = (s - RET0 - 3) // 2
                    if (s - RET0) % 2 == 1 and 0 <= hd < HEADS:
                        eng.wait_ge(gated, l * HEADS + (hd + 1))
                        eng.activation(gh[:, RET_C + hd, qf:T], rn[:, qf:T], ACT.Copy).then_inc(rh_ready, 1)
                    hd = (s - RET0 - 1) // 2
                    if (s - RET0) % 2 == 1 and 0 <= hd < HEADS:
                        eng.wait_ge(ret_o, l * HEADS + (hd + 1))
                        eng.activation(ro[:, qf:T], bank[:, 5, qf:T], ACT.Copy).then_inc(ro_ready, 1)
                        eng.activation(rs[:, qf:T], bank[:, 5, qf:T], ACT.Square).then_inc(rs_ready, 1)
                    hd = (s - RET0 - 2) // 2
                    if (s - RET0) % 2 == 0 and 0 <= hd < HEADS:
                        eng.wait_ge(ret_var, l * HEADS + (hd + 1))
                        eng.activation(rr[:, qf:T], bank[:, 5, qf:T], ACT.Ln, bias=eps[:, 0:1]).then_inc(ln_ready, 1)
                        eng.wait_ge(ln_ready, l * HEADS + (hd + 1))
                        eng.activation(rr[:, qf:T], rr[:, qf:T], ACT.Exp, scale=-0.5).then_inc(rr_ready, 1)
                    hd = (s - SB0) // 2
                    if (s - SB0) % 2 == 0 and 0 <= hd < HEADS:
                        eng.wait_ge(z_done, l * HEADS + (hd + 1))
                        eng.activation(sa[:, qf:], bank[:, 6, qf:SCORES], ACT.Abs).then_inc(sa_step, 1)
                        eng.wait_ge(sa_step, l * 3 * HEADS + (3 * hd + 1))
                        eng.activation(sa[:, qf:], sa[:, qf:], ACT.Exp, scale=-1.0).then_inc(sa_step, 1)
                        eng.wait_ge(sa_step, l * 3 * HEADS + (3 * hd + 2))
                        eng.activation(sa[:, qf:], sa[:, qf:], ACT.Ln, bias=1.0).then_inc(sa_step, 1)
                    hd = (s - SB0 - 1) // 2
                    if (s - SB0) % 2 == 1 and 0 <= hd < HEADS:
                        eng.wait_ge(cum_done, l * HEADS + (hd + 1))
                        eng.activation(pa[:, qf:], bank[:, 6, qf:SCORES], ACT.Exp).then_inc(pa_ready, 1)
                    hd = (s - SB0 - 2) // 2
                    if (s - SB0) % 2 == 0 and 0 <= hd < HEADS and hd % 2:
                        eng.wait_ge(sbo_done, l * HEADS + (hd + 1))
                        eng.activation(gh[:, SB_C + hd // 2, qf:T], bank[:, 7, qf:T], ACT.Copy).then_inc(sbh_ready, 1)
                    k = s - (SB0 + 2 * HEADS)
                    if 0 <= k < PAIRS:
                        for gate, u0 in ((ga, U_GA), (gb, U_GB)):
                            eng.wait_ge(unit_evicted, l * UNITS + (u0 + k + 1))
                            eng.activation(gate[:, 2 * k:2 * k + 2, qf:T], gate[:, 2 * k:2 * k + 2, qf:T],
                                           ACT.Sigmoid).then_inc(sig_ready, 1)
                    if S_Y <= s < S_OUT and Y_STEPS[s - S_Y][1] == "s":
                        k = Y_STEPS[s - S_Y][2]
                        eng.wait_ge(y_merged, l * PAIRS + (k + 1))
                        c = MERGE_C + 2 * k
                        eng.activation(gh[:, c:c + 2, qf:T], ga[:, 2 * k:2 * k + 2, qf:T], ACT.Copy).then_inc(yh_ready, 1)
                    if s == S_OUT - 1:
                        eng.preload_act_table_set("sqrt_and_others")

            def layer(l):
                ffn(l, 0)
                mixer(l)
                ffn(l, 1)

            eng.dma_start(gain[:, :, :], gains).then_inc(gains_in, 16)
            for p in range(PAIRS):
                eng.dma_start(h[:, 2 * p:2 * p + 2, :], h_in[:, 2 * p:2 * p + 2, :]).then_inc(h_loaded[p], 16)
            eng.dma_start(gn_gain[:, :, :], gn_gains).then_inc(gn_gains_in, 16)
            eng.preload_act_table_set("sqrt_and_others")
            for j in range(RING):
                split_hi(j, j, first=True)
                hi_of_h(0, j, 0, loaded=True)
            eng.wait_ge(pads_ready, 3)
            layers(eng, layer)
            rms(3 * DEPTH, N_META)

        @block.vector
        def _(eng):
            def split_lo(n, slot):
                eng.wait_ge(hi_ready, n + 1)
                eng.tensor_tensor(w_lo[:, slot, :], raw[:, slot, :], w_hi[:, slot, :].bitcast(F32),
                                  ALU.subtract).then_inc(lo_ready, 1)

            def scale_h(rnd, p, q0):
                if not (isinstance(rnd, int) and rnd == 0 and p < 2):
                    eng.wait_ge(x_ready, rnd * PAIRS + (p - 1))
                for c in range(2):
                    eng.tensor_scalar(xg[:, p % 2, c, q0:T], h[:, 2 * p + c, q0:T], gain[:, bass.ds(rnd, 1), 2 * p + c],
                                      None, ALU.mult).then_inc(x_scaled, 1)

            def lo_of_h(rnd, p, q0):
                c = 2 * p
                eng.wait_ge(xh_ready, rnd * PAIRS + (p + 1))
                eng.tensor_tensor(xl[:, c:c + 2, q0:T], xg[:, p % 2, :, q0:T], xh[:, c:c + 2, q0:T].bitcast(F32),
                                  ALU.subtract).then_inc(x_ready, 1)

            def norm_factor(rnd, q0):
                eng.wait_ge(ssum_done, rnd + 1)
                eng.tensor_scalar(ms[:, q0:T], bank[:, 4, q0:T], 1.0 / DC, EPS, ALU.mult, ALU.add).then_inc(ms_ready, 1)
                eng.wait_ge(rms_ready, rnd + 1)
                eng.reciprocal(r[:, q0:T], r[:, q0:T]).then_inc(r_ready, 1)

            def update_h(rnd, p, b, factor, q0, final=False):
                c = 2 * p
                eng.scalar_tensor_tensor(h[:, c:c + 2, q0:T], pair(b, q0), factor, h[:, c:c + 2, q0:T],
                                         ALU.mult, ALU.add).then_inc(h_new, 1)
                if not final:
                    eng.wait_ge(h_new, (rnd - 1) * PAIRS + (p + 1))
                    scale_h(rnd, p, q0)
                    lo_of_h(rnd, p, q0)

            def ffn(l, f):
                fi = l * 2 + f
                off = 0 if f == 0 else FFN + MIX
                base = l * PER_LAYER + off
                last = first_query(l) > 0 and f == 1
                q0 = first_query(l) if f else 0
                norm_factor(l * 3 + 2 * f, q0)
                with eng.Fori(0, ITERS) as it:
                    i = fi * ITERS + it
                    for j in range(4):
                        if j == 1:
                            eng.wait_ge(r_ready, l * 3 + 2 * f + 1)
                            eng.wait_ge(piece_done, base + it * 4 + 2)
                            eng.tensor_tensor(scl[:, :, q0:T], pair(0, q0), twice(r, q0), ALU.mult).then_inc(gate_scaled, 1)
                        if j == 3:
                            eng.wait_ge(gate_act, i + 1)
                            eng.wait_ge(g_ready, i + 1)
                            eng.wait_ge(piece_done, base + it * 4 + 4)
                            eng.tensor_tensor(gv[:, :, q0:T], pair(2, q0), act[:, :, q0:T], ALU.mult).then_inc(up_gated, 1)
                        split_lo(base + it * 4 + (j + RING), (off + j) % RING)
                    eng.wait_ge(up_gated, i + 1)
                    eng.tensor_tensor(gv[:, :, q0:T], gv[:, :, q0:T], twice(r, q0), ALU.mult).then_inc(g_val, 1)
                    eng.wait_ge(gh_ready, i + 1)
                    eng.tensor_tensor(gl[:, bass.ds(it * 2, 2), q0:T], gv[:, :, q0:T],
                                      gh[:, bass.ds(it * 2, 2), q0:T].bitcast(F32), ALU.subtract).then_inc(g_ready, 1)
                for q in range(QUADS):
                    for c in range(ITERS):
                        s = GU + q * ITERS + c
                        if c >= ITERS - 2:
                            k = c - (ITERS - 2)
                            eng.wait_ge(piece_done, base + (s + 1))
                            update_h(l * 3 + 2 * f + 1, 2 * q + k, 4 * q + 2 * k, 0.5, q0, final=last)
                        if not last or s + RING < FFN:
                            split_lo(base + (s + RING), (off + s) % RING)

            def mixer(l):
                base = l * PER_LAYER + FFN
                qf = first_query(l)
                norm_factor(l * 3 + 1, 0)
                eng.wait_ge(table_in, 16)
                eng.wait_ge(gn_gains_in, 16)
                eng.wait_ge(r_ready, l * 3 + 2)

                def rotary(k):
                    return (rq[:, 2 * k:2 * k + 2, qf:T], qf) if k < U_K else (rk[:, 2 * (k - U_K):2 * (k - U_K) + 2, 0:T], 0)

                for s in range(MIX):
                    u = s // 2
                    if s % 2 == 0 and 0 < u <= U_V:
                        k = u - 1
                        dst, q0 = rotary(k)
                        eng.wait_ge(swapped, l * 4 * U_V + 4 * (k + 1))
                        eng.tensor_tensor(act[:, :, q0:T], act[:, :, q0:T], twice(sin, q0), ALU.mult).then_inc(rot_sin, 1)
                        eng.wait_ge(rot_sin, l * U_V + (k + 1))
                        eng.wait_ge(rot_cos, l * U_V + (k + 1))
                        eng.tensor_tensor(dst, dst, act[:, :, q0:T], ALU.add).then_inc(rotated, 1)
                    hd = (s - RET0 - 3) // 2
                    if (s - RET0) % 2 == 1 and 0 <= hd < HEADS:
                        eng.wait_ge(rr_ready, l * HEADS + (hd + 1))
                        if hd:
                            eng.wait_ge(ret_ready, l * HEADS + hd)
                        eng.tensor_tensor(rn[:, qf:T], ro[:, qf:T], rr[:, qf:T], ALU.mult).then_inc(rn_ready, 1)
                        eng.wait_ge(rn_ready, l * HEADS + (hd + 1))
                        eng.wait_ge(rg_ready, l * PAIRS + (hd // 2 + 1))
                        eng.scalar_tensor_tensor(rn[:, qf:T], rn[:, qf:T], gn_gain[:, bass.ds(l, 1), hd], rg[:, hd, qf:T],
                                                 ALU.mult, ALU.mult).then_inc(gated, 1)
                    hd = (s - RET0 - 4) // 2
                    if (s - RET0) % 2 == 0 and 0 <= hd < HEADS:
                        eng.wait_ge(rh_ready, l * HEADS + (hd + 1))
                        eng.tensor_tensor(gl[:, RET_C + hd, qf:T], rn[:, qf:T], gh[:, RET_C + hd, qf:T].bitcast(F32),
                                          ALU.subtract).then_inc(ret_ready, 1)
                    hd = (s - SB0 - 1) // 2
                    if (s - SB0) % 2 == 1 and 0 <= hd < HEADS:
                        eng.wait_ge(sa_step, l * 3 * HEADS + 3 * (hd + 1))
                        eng.scalar_tensor_tensor(sp[:, qf:], bank[:, 6, qf:SCORES], 0.0, sa[:, qf:],
                                                 ALU.max, ALU.add).then_inc(sp_ready, 1)
                    hd = (s - SB0 - 3) // 2
                    if (s - SB0) % 2 == 1 and 0 <= hd < HEADS and hd % 2:
                        eng.wait_ge(sbh_ready, l * PAIRS + (hd // 2 + 1))
                        c = SB_C + hd // 2
                        eng.tensor_tensor(gl[:, c, qf:T], bank[:, 7, qf:T], gh[:, c, qf:T].bitcast(F32),
                                          ALU.subtract).then_inc(sb_ready, 1)
                    if S_Y < s < S_OUT:
                        j, kind, k, half = Y_STEPS[s - S_Y - 1]
                        if kind == "r" and half:
                            eng.wait_ge(sig_ready, l * 2 * PAIRS + (2 * k + 2))
                            c = 2 * k
                            eng.tensor_tensor(ga[:, c:c + 2, qf:T], pair(Y_BANKS[j % 3], qf), ga[:, c:c + 2, qf:T],
                                              ALU.mult).then_inc(unit_evicted, 1)

                    def merged_lo(k):
                        c = MERGE_C + 2 * k
                        eng.wait_ge(yh_ready, l * PAIRS + (k + 1))
                        eng.tensor_tensor(gl[:, c:c + 2, qf:T], ga[:, 2 * k:2 * k + 2, qf:T],
                                          gh[:, c:c + 2, qf:T].bitcast(F32), ALU.subtract).then_inc(y_ready, 1)

                    if S_Y < s < S_OUT and Y_STEPS[s - S_Y - 1][1] == "s":
                        merged_lo(Y_STEPS[s - S_Y - 1][2])

                    eng.wait_ge(piece_done, base + (s + 1))
                    if s % 2 and u < U_Y:
                        q0 = 0 if U_K <= u < U_G or U_SK <= u < U_GA else qf
                        res, rb = pair(2 * (u % 2), q0), twice(r, q0)
                        if u < U_V:
                            eng.tensor_tensor(scl[:, :, q0:T], res, rb, ALU.mult).then_inc(unit_evicted, 1)
                            eng.wait_ge(unit_evicted, l * UNITS + (u + 1))
                            eng.tensor_tensor(rotary(u)[0], scl[:, :, q0:T], twice(cos, q0), ALU.mult).then_inc(rot_cos, 1)
                        elif u < U_SQ or U_SV <= u < U_GA:
                            if U_V < u <= U_G:
                                eng.wait_ge(v_turned, l * 6 + (u - U_V))
                            if U_G < u < U_SQ:
                                eng.wait_ge(rg_ready, l * PAIRS + (u - U_G))
                            if u == U_SV:
                                eng.wait_ge(rg_ready, l * PAIRS + PAIRS)
                            if u == U_SV + 1:
                                eng.wait_ge(v_turned, l * 6 + 5)
                            eng.tensor_tensor(scl[:, :, q0:T], res, rb, ALU.mult).then_inc(unit_evicted, 1)
                        elif u < U_SK:
                            c = 2 * (u - U_SQ)
                            eng.scalar_tensor_tensor(sq[:, c:c + 2, q0:T], res, DK ** -0.5, rb,
                                                     ALU.mult, ALU.mult).then_inc(unit_evicted, 1)
                        else:
                            dst, u0 = (sk, U_SK) if u < U_SV else (ga, U_GA) if u < U_GB else (gb, U_GB)
                            c = 2 * (u - u0)
                            eng.tensor_tensor(dst[:, c:c + 2, q0:T], res, rb, ALU.mult).then_inc(unit_evicted, 1)
                    if S_Y <= s < S_OUT and Y_STEPS[s - S_Y][1] == "s":
                        j, _, k, _ = Y_STEPS[s - S_Y]
                        c = 2 * k
                        eng.wait_ge(sig_ready, l * 2 * PAIRS + (2 * k + 2))
                        eng.tensor_tensor(gb[:, c:c + 2, qf:T], pair(Y_BANKS[j % 3], qf), gb[:, c:c + 2, qf:T],
                                          ALU.mult).then_inc(unit_evicted, 1)
                        eng.wait_ge(unit_evicted, l * UNITS + (U_Y + j + 1))
                        eng.tensor_tensor(ga[:, c:c + 2, qf:T], ga[:, c:c + 2, qf:T], gb[:, c:c + 2, qf:T],
                                          ALU.add).then_inc(y_merged, 1)
                        if s == S_OUT - 1:
                            merged_lo(k)
                    if s >= S_OUT and s % 2:
                        p = (s - S_OUT) // 2
                        update_h(l * 3 + 2, p, OUT_BANKS[p], 1.0, qf)
                    split_lo(base + (s + RING), (FFN + s) % RING)
                    hd = (s - RET0) // 2
                    if (s - RET0) % 2 == 0 and 0 <= hd < HEADS:
                        c = C_DECAY + hd * SCORES
                        if hd:
                            eng.wait_ge(ret_o, l * HEADS + hd)
                        eng.wait_ge(ret_scores, l * HEADS + (hd + 1))
                        eng.tensor_tensor(dec[:, qf:], bank[:, 4, qf:SCORES], table[:, c + qf:c + SCORES],
                                          ALU.mult).then_inc(ret_decayed, 1)

            def layer(l):
                ffn(l, 0)
                mixer(l)
                ffn(l, 1)

            eng.memset(gv[:, :, :], 0.0).then_inc(g_ready, 1)
            eng.wait_ge(gains_in, 16)
            for p in range(PAIRS):
                eng.wait_ge(h_loaded[p], 16)
                scale_h(0, p, 0)
                split_lo(p, p)
                lo_of_h(0, p, 0)
            eng.wait_ge(squares_in, 16)
            eng.tensor_copy(neg_r[:, :], neg).then_inc(masks_ready, 1)
            eng.tensor_copy(ident_r[:, :], ident).then_inc(masks_ready, 1)
            layers(eng, layer)
            eng.wait_ge(sq_ready, 3 * DEPTH * PAIRS + PAIRS)
            for c in range(DC):
                eng.tensor_scalar(h[:, c, N_META:T], h[:, c, N_META:T], gain[:, 3 * DEPTH, c:c + 1], None,
                                  ALU.mult).then_inc(scaled_out, 1)
            eng.wait_ge(scaled_out, DC)
            norm_factor(3 * DEPTH, N_META)
            eng.wait_ge(r_ready, 3 * DEPTH + 1)
            for p in range(PAIRS - 1):
                eng.tensor_tensor(h[:, 2 * p:2 * p + 2, N_META:T], h[:, 2 * p:2 * p + 2, N_META:T], twice(r, N_META),
                                  ALU.mult).then_inc(out_ready, 1)

        @block.tensor
        def _(pe):
            def use(n, slot, blocks, before=None):
                pe.wait_ge(lo_ready, n + 1)
                for b, (hi, lo, out, first, last) in enumerate(blocks):
                    if before and b in before:
                        before[b]()
                    wh = w_hi[:, slot, b * P:(b + 1) * P]
                    wl = w_lo[:, slot, b * P:(b + 1) * P]
                    pe.matmul(out, wh, hi, start=first, stop=False)
                    pe.matmul(out, wh, lo, start=False, stop=False)
                    mm = pe.matmul(out, wl, hi, start=False, stop=last)
                mm.then_inc(piece_done, 1)

            def k_half(src_h, src_l, half, b, q0, halves=2, c0=0):
                return [(src_h[:, c0 + 4 * half + k, q0:T], src_l[:, c0 + 4 * half + k, q0:T], bank[:, b + m, q0:T],
                         half == 0 and k == 0, half == halves - 1 and k == 3) for k in range(4) for m in range(2)]

            def sum_of_squares(rnd, q0, final=False):
                pe.wait_ge(squares_in, 16)
                pe.wait_ge(ssq_added, rnd * ADDS + (ADDS - 1 if final else ADDS))
                pe.matmul(bank[:, 4, q0:T], ones, ssq[:, 0, q0:T], start=True, stop=False)
                mm = pe.matmul(bank[:, 4, q0:T], ones, ssq[:, 1, q0:T], start=False, stop=not final)
                if final:
                    pe.wait_ge(sq_ready, rnd * PAIRS + PAIRS)
                    pe.matmul(bank[:, 4, q0:T], ones, sqh[:, 0, q0:T], start=False, stop=False)
                    mm = pe.matmul(bank[:, 4, q0:T], ones, sqh[:, 1, q0:T], start=False, stop=True)
                mm.then_inc(ssum_done, 1)

            def first_unit(rnd, piece, q0, b):
                def wait_x(p):
                    pe.wait_ge(x_ready, rnd * PAIRS + (p + 1))

                wait_x(0)
                piece(0, {0: lambda: wait_x(2) if b else None, 4: lambda: wait_x(1)})
                piece(1, {0: lambda: wait_x(2), 4: lambda: wait_x(3)})

            def ffn(l, f):
                fi = l * 2 + f
                off = 0 if f == 0 else FFN + MIX
                base = l * PER_LAYER + off
                q0 = first_query(l) if f else 0

                def gate(n, half, before=None):
                    use(n, (off + half) % RING, k_half(xh, xl, half, 0, q0), before)

                def up(n, half, before=None):
                    use(n, (off + 2 + half) % RING, k_half(xh, xl, half, 2, q0), before)

                first_unit(l * 3 + 2 * f, lambda half, before: gate(base + half, half, before), q0, f)
                up(base + 2, 0, {2: lambda: sum_of_squares(l * 3 + 2 * f, q0)})
                up(base + 3, 1)
                with pe.Fori(1, ITERS) as it:
                    pe.wait_ge(gate_scaled, fi * ITERS + it)
                    gate(base + it * 4, 0)
                    gate(base + it * 4 + 1, 1)
                    pe.wait_ge(up_gated, fi * ITERS + it)
                    up(base + it * 4 + 2, 0)
                    up(base + it * 4 + 3, 1)
                pe.wait_ge(gate_scaled, fi * ITERS + ITERS)
                for q in range(QUADS):
                    for c in range(ITERS):
                        if q == 0 and c < ITERS - 1:
                            pe.wait_ge(g_ready, fi * ITERS + (c + 2 if c < ITERS - 2 else ITERS + 1))
                        if c < ITERS - 2:
                            blocks = [(2 * c + k, m, c == 0 and k == 0, False) for m in range(4) for k in range(2)]
                        else:
                            m0, k0 = 2 * (c - (ITERS - 2)), FC - 4
                            blocks = [(k0 + k, m0 + m, False, k == 3) for k in range(4) for m in range(2)]
                        s = GU + q * ITERS + c
                        use(base + s, (off + s) % RING,
                            [(gh[:, k, q0:T], gl[:, k, q0:T], bank[:, 4 * q + m, q0:T], first, last)
                             for k, m, first, last in blocks],
                            {4: lambda: pe.wait_ge(up_gated, fi * ITERS + ITERS)} if q == c == 0 else None)

            def turn_values(l, b, centred):
                for m in range(2):
                    for j, (t0, n) in enumerate(TOK):
                        out = bank[0:n, b, 256 * j + P * m:256 * j + P * m + P] if j < 2 else bank[0:n, b + 1, P * m:P * m + P]
                        if centred:
                            mm = pe.matmul(out, scl[:, m, t0:t0 + n], centre, start=True, stop=True)
                        else:
                            mm = pe.transpose(out, scl[:, m, t0:t0 + n], ident)
                mm.then_inc(v_turned, 1)

            def mixer(l):
                base = l * PER_LAYER + FFN
                rnd = l * 3 + 1
                qf = first_query(l)

                def piece(s, blocks, before=None):
                    use(base + s, (FFN + s) % RING, blocks, before)

                first_unit(rnd, lambda half, before: piece(half, k_half(xh, xl, half, 0, qf), before), 0, 0)
                for s in range(2, MIX):
                    u = s // 2
                    if s < S_Y:
                        if s % 2 == 0 and u >= 2:
                            pe.wait_ge(unit_evicted, l * UNITS + (u - 1))
                        q0 = 0 if U_K <= u < U_G or U_SK <= u < U_GA else qf
                        piece(s, k_half(xh, xl, s % 2, 2 * (u % 2), q0),
                              {2: lambda: sum_of_squares(rnd, 0)} if s == 2 else None)
                    elif s < S_OUT:
                        j, kind, k, half = Y_STEPS[s - S_Y]
                        if s == S_Y:
                            pe.wait_ge(ret_ready, l * HEADS + HEADS)
                        if half == 0 and j != 2:
                            pe.wait_ge(unit_evicted, l * UNITS + (U_Y - 1 + j if j < 2 else U_Y + j - 2))
                        if j == 2:
                            pe.wait_ge(sb_ready, l * PAIRS + PAIRS)
                        if kind == "r":
                            piece(s, k_half(gh, gl, half, Y_BANKS[j % 3], qf, c0=RET_C))
                        else:
                            piece(s, k_half(gh, gl, 0, Y_BANKS[j % 3], qf, halves=1, c0=SB_C))
                    else:
                        p, half = (s - S_OUT) // 2, s % 2
                        if half == 0 and p:
                            pe.wait_ge(unit_evicted, l * UNITS + (U_Y + OUT_AFTER[p] + 1))
                        blocks = k_half(gh, gl, half, OUT_BANKS[p], qf, c0=MERGE_C)
                        if p == 0:
                            piece(s, blocks, {0: lambda: pe.wait_ge(y_ready, l * PAIRS + (2 * half + 1)),
                                              4: lambda: pe.wait_ge(y_ready, l * PAIRS + (2 * half + 2))})
                        else:
                            piece(s, blocks)
                    for u0, cnt, first, b in ((U_V, 4, 0, 4), (U_SV, 2, 4, 6)):
                        k = s // 2 - 1 - u0
                        if s % 2 == 0 and 0 <= k < cnt:
                            if s == 2 * U_V + 2:
                                pe.wait_ge(squares_in, 16)
                            pe.wait_ge(unit_evicted, l * UNITS + (u0 + k + 1))
                            if k:
                                pe.wait_ge(v_ready, l * 12 + 2 * (first + k))
                            turn_values(l, b, u0 == U_V)
                    hd = (s - RET0 - 1) // 2
                    if (s - RET0) % 2 == 1 and 0 <= hd < HEADS:
                        pe.wait_ge(ret_decayed, l * HEADS + (hd + 1))
                        if hd:
                            pe.wait_ge(ln_ready, l * HEADS + hd)
                        for i, (t0, cnt) in enumerate(TOK):
                            q = max(t0, qf)
                            c = SEG[i] + q - t0
                            mm = pe.matmul(bank[:, 5, q:T], rv[0:cnt, i, hd * DV:(hd + 1) * DV],
                                           dec[0:cnt, c:c + T - q], start=(i == 0), stop=(i == 2))
                        mm.then_inc(ret_o, 1)
                    hd = (s - RET0 - 2) // 2
                    if (s - RET0) % 2 == 0 and 0 <= hd < HEADS:
                        pe.wait_ge(rs_ready, l * HEADS + (hd + 1))
                        pe.matmul(bank[:, 5, qf:T], ones, rs[:, qf:T], start=True, stop=True).then_inc(ret_var, 1)
                    hd = (s - RET0) // 2
                    if (s - RET0) % 2 == 0 and 0 <= hd < HEADS:
                        if hd == 0:
                            pe.wait_ge(pads_ready, 3)
                            pe.wait_ge(rotated, l * U_V + U_V)
                            pe.wait_ge(v_ready, l * 12 + 8)
                        f0 = DK * (hd % 2)
                        for i, (t0, cnt) in enumerate(TOK):
                            q = max(t0, qf)
                            c = SEG[i] + q - t0
                            mm = pe.matmul(bank[:, 4, c:c + T - q], rk[f0:f0 + DK, hd // 2, t0:t0 + P],
                                           rq[f0:f0 + DK, hd // 2, q:T], start=(i == 0), stop=True, skip_group_check=True)
                        mm.then_inc(ret_scores, 1)
                    hd = (s - SB0 - 2) // 2
                    if (s - SB0) % 2 == 0 and 0 <= hd < HEADS:
                        pe.wait_ge(pa_ready, l * HEADS + (hd + 1))
                        if hd >= 2 and hd % 2 == 0:
                            pe.wait_ge(sb_ready, l * PAIRS + hd // 2)
                        f0 = DK * (hd % 2)
                        for i, (t0, cnt) in enumerate(TOK):
                            q = max(t0, qf)
                            c = SEG[i] + q - t0
                            mm = pe.matmul(bank[f0:f0 + DK, 7, q:T], sv[0:cnt, i, hd * DK:(hd + 1) * DK],
                                           pa[0:cnt, c:c + T - q], start=(i == 0), stop=(i == 2))
                        mm.then_inc(sbo_done, 1)
                    hd = (s - SB0 - 1) // 2
                    if (s - SB0) % 2 == 1 and 0 <= hd < HEADS:
                        pe.wait_ge(sp_ready, l * HEADS + (hd + 1))
                        def add_sum(out, weights, summed):
                            return pe.matmul(out, weights, summed, start=False, stop=True, skip_group_check=True)

                        for i, (t0, cnt) in enumerate(TOK):
                            q = max(t0, qf)
                            c = SEG[i] + q - t0
                            add_sum(bank[:, 6, c:c + T - q], cum, sp[:, c:c + T - q])
                        add_sum(bank[:, 6, P:SEG[1]], allneg, sp[:, SEG[1]:SEG[2]])
                        n = TOK[2][1]
                        both = strided_pair(SEG[1] - n, T - P, n)
                        add_sum(both, allneg, sp[:, SEG[2]:SCORES].unsqueeze(1).to_broadcast([P, 2, n])).then_inc(cum_done, 1)
                    hd = (s - SB0) // 2
                    if (s - SB0) % 2 == 0 and 0 <= hd < HEADS:
                        if hd == 0:
                            pe.wait_ge(masks_ready, 2)
                            pe.wait_ge(v_ready, l * 12 + 12)
                        f0 = DK * (hd % 2)
                        for i, (t0, cnt) in enumerate(TOK):
                            q = max(t0, qf)
                            c = SEG[i] + q - t0
                            pe.matmul(bank[:, 6, c:c + T - q], sk[f0:f0 + DK, hd // 2, t0:t0 + P],
                                      sq[f0:f0 + DK, hd // 2, q:T], start=(i == 0), stop=True, skip_group_check=True)
                        pe.matmul(strided_pair(0, T, P), ident_r[:, :],
                                  neg_r[:, :].unsqueeze(1).to_broadcast([P, 2, P]),
                                  start=False, stop=True, skip_group_check=True)
                        pe.matmul(bank[:, 6, SEG[2]:SCORES], ident_r[:, :], neg_r[:, 0:TOK[2][1]],
                                  start=False, stop=True, skip_group_check=True).then_inc(z_done, 1)

            def layer(l):
                ffn(l, 0)
                mixer(l)
                ffn(l, 1)

            layers(pe, layer)
            sum_of_squares(3 * DEPTH, N_META, True)


def piece_stream(a):
    pieces = []

    def k_halves(w, c0, cols, halves=2):
        for half in range(halves):
            part = w[half * 4 * P:(half + 1) * 4 * P, c0:c0 + cols]
            pieces.append(part.reshape(4, P, cols).transpose(1, 0, 2).reshape(P, PIECE))

    def ffn(gu, down):
        for it in range(ITERS):
            k_halves(gu, it * 2 * P, 2 * P)
            k_halves(gu, D_FF + it * 2 * P, 2 * P)
        for q in range(QUADS):
            for c in range(ITERS - 2):
                part = down[c * 2 * P:(c + 1) * 2 * P, q * 4 * P:(q + 1) * 4 * P]
                pieces.append(part.reshape(2, P, 4, P).transpose(1, 2, 0, 3).reshape(P, PIECE))
            for half in range(2):
                part = down[(FC - 4) * P:, (q * 4 + half * 2) * P:(q * 4 + half * 2 + 2) * P]
                pieces.append(part.reshape(4, P, 2 * P).transpose(1, 0, 2).reshape(P, PIECE))

    for l in range(DEPTH):
        ffn(a["ffn1_w_gu"][l], a["ffn1_w_down"][l])
        for u in range(U_Y):
            k_halves(a["w_in"][l], u * 2 * P, 2 * P)
        for kind, pr in Y_UNITS:
            if kind == "r":
                k_halves(a["w_ret_proj"][l], pr * 2 * P, 2 * P)
            else:
                k_halves(a["w_sb_proj"][l], pr * 2 * P, 2 * P, halves=1)
        for u in range(PAIRS):
            k_halves(a["w_out"][l], u * 2 * P, 2 * P)
        ffn(a["ffn2_w_gu"][l], a["ffn2_w_down"][l])
    return np.stack(pieces)


def constants():
    f = np.float32
    row = np.arange(P)
    freq = f(10000.0) ** (-np.arange(0, DK, 2, dtype=f) / f(DK))
    angle = (np.arange(T, dtype=f)[None, :] * freq[row % 32][:, None]).astype(f)
    sign = np.where(row % DK < DK // 2, -1.0, 1.0)[:, None]
    tables = [np.cos(angle), sign * np.sin(angle)]
    for hd in range(HEADS):
        log_gamma = np.log(1.0 - 2.0 ** (-5.0 - hd))
        for t0, _ in TOK:
            diff = np.arange(T - t0)[None, :] - row[:, None]
            tables.append(np.where(diff >= 0, np.exp(log_gamma * np.maximum(diff, 0)), 0.0) * DK ** -0.5)
    key, query = row[:, None], row[None, :]
    squares = [np.full((P, P), 1.0 / P), np.eye(P), np.eye(P) - 1.0 / P, np.where(key >= query, NEG, 0.0),
               np.where(key >= query, -1.0, 0.0), np.full((P, P), -1.0)]
    return [np.ascontiguousarray(np.concatenate(x, axis=1), dtype=f) for x in (tables, squares)]


def kernel(**inputs):
    import concourse.bacc as bacc
    from concourse.bass_utils import run_bass_kernel_spmd

    a = {k: np.asarray(v) for k, v in inputs.items()}
    tokens = np.concatenate([a["meta"], a["x"][0]], axis=0)
    norms = [n for l in range(DEPTH) for n in (a["ffn1_norm"][l], a["mix_norm"][l], a["ffn2_norm"][l])]
    gains = np.stack(norms + [a["final_norm"]])
    arrays = {
        "stream": np.ascontiguousarray(piece_stream(a)),
        "tokens": np.ascontiguousarray(tokens.T.reshape(DC, P, T).transpose(1, 0, 2)),
        "gains": np.ascontiguousarray(gains.reshape(3 * DEPTH + 1, DC, P).transpose(2, 0, 1)),
        "gn_gains": np.ascontiguousarray(a["ret_gn"].reshape(DEPTH, HEADS, P).transpose(2, 0, 1)),
    }
    arrays["tables"], arrays["squares"] = constants()
    nc = bacc.Bacc("TRN2", target_bir_lowering=False, num_devices=1)
    args = [nc.dram_tensor(name, v.shape, mybir.dt.from_np(v.dtype), kind="ExternalInput").ap()
            for name, v in arrays.items()]
    out = nc.dram_tensor("out", (P, DC, SEQ), F32, kind="ExternalOutput").ap()
    trunk(nc, *args, out)
    got = run_bass_kernel_spmd(nc, [arrays], core_ids=[0]).results[0]["out"]
    return np.ascontiguousarray(got.transpose(2, 1, 0)).reshape(1, SEQ, D)
```

```python
from contextlib import ExitStack

import concourse.bass as bass
import numpy as np
from concourse import mybir

F32 = mybir.dt.float32
F32R = mybir.dt.float32r
ALU = mybir.AluOpType
ACT = mybir.ActivationFunctionType

P = 128
D = 1024
DEPTH = 2
N_META = 16
SEQ = 256
T = N_META + SEQ
HEADS = 8
DK = 64
DV = 128
D_FF = 2816
EPS = 1e-6
DC = D // P
FC = D_FF // P
ITERS = FC // 2
BLOCKS = 8
PIECE = BLOCKS * P
RING = 4
TOK = [(0, P), (P, P), (2 * P, T - 2 * P)]
SEG = [0, T, T + (T - P)]
SCORES = T + (T - P) + (T - 2 * P)
PADT = 3 * P

GU = 4 * ITERS
QUADS = 2
FFN = GU + QUADS * ITERS
U_Q, U_K, U_V, U_G, U_SQ, U_SK, U_SV, U_GA, U_GB, U_Y = 0, 2, 4, 8, 12, 14, 16, 18, 22, 26
Y_UNITS = [("r", 0), ("r", 1), ("r", 2), ("s", 0), ("s", 1), ("s", 2), ("r", 3), ("s", 3)]
Y_STEPS = [(j, kind, pr, half) for j, (kind, pr) in enumerate(Y_UNITS) for half in range(2 if kind == "r" else 1)]
Y_BANKS = [0, 2, 4]
S_Y = 2 * U_Y
S_OUT = S_Y + len(Y_STEPS)
MIX = S_OUT + 8
OUT_BANKS = [6, 4, 0, 2]
OUT_AFTER = [None, 5, 6, 7]
PER_LAYER = 2 * FFN + MIX
UNITS = U_Y - U_V + len(Y_UNITS)
PAIRS = DC // 2
ADDS = PAIRS - 1
RET0, SB0 = 2 * U_SQ, 37
NEG = -2.0 ** 100

C_COS, C_SIN, C_DECAY = 0, T, 2 * T
C_ONES, C_IDENT, C_NEG, C_CUM, C_ALL = (P * i for i in range(5))
SQUARES = 5 * P


def trunk(nc, stream, h_in, gains, gn_gains, tables, squares, h_out):
    with ExitStack() as ctx:
        def sb(name, shape, dt=F32):
            return ctx.enter_context(nc.sbuf_tensor(name, shape, dt))

        def sem(name):
            return ctx.enter_context(nc.semaphore(name))

        raw = sb("raw", [P, RING, PIECE])
        w_hi = sb("w_hi", [P, RING, PIECE], F32R)
        w_lo = sb("w_lo", [P, RING, PIECE], F32R)
        h = sb("h", [P, DC, T])
        xh = sb("xh", [P, DC, T], F32R)
        xl = sb("xl", [P, DC, T], F32R)
        gh = sb("gh", [P, FC, T], F32R)
        gl = sb("gl", [P, FC, T], F32R)
        RET_C, SB_C, MERGE_C = 0, 8, 12
        rq = sb("rq", [P, 4, T])
        rk = sb("rk", [P, 4, T])
        rv = sb("rv", [P, 3, D])
        rg = sb("rg", [P, DC, T])
        sq = sb("sq", [P, 4, T])
        sk = sb("sk", [P, 4, PADT])
        sv = sb("sv", [P, 3, D // 2])
        ga = rg
        gb = rv[:, :, :].rearrange("p a b -> p (a b)")[:, 0:DC * T].rearrange("p (c t) -> p c t", t=T)
        table = sb("table", [P, C_DECAY + HEADS * SCORES])
        square = sb("square", [P, C_NEG])
        square_r = sb("square_r", [P, SQUARES], F32R)
        vsum = sb("vsum", [P, 3, 2])
        gain = sb("gain", [P, 3 * DEPTH + 1, DC])
        gn_gain = sb("gn_gain", [P, DEPTH, HEADS])
        eps = sb("eps", [P, 1])
        scl = sb("scl", [P, 2, T])
        act = sb("act", [P, 2, T])
        gv = sb("gv", [P, 2, T])
        xg = sb("xg", [P, 2, 2, T])
        sqh = sb("sqh", [P, 2, T])
        ssq = sb("ssq", [P, 2, T])
        ms = sb("ms", [P, T])
        r = sb("r", [P, T])
        dec = sb("dec", [P, SCORES])
        ro = sb("ro", [P, T])
        rs, rr = gv[:, 0, :], gv[:, 1, :]
        rs_hi, rs_lo = gh[:, MERGE_C, :], gl[:, MERGE_C, :]
        r_cos, r_sin = scl[:, 0, :], scl[:, 1, :]
        rn = xg[:, 1, 0, :]
        sa = ssq[:, :, :].rearrange("p a t -> p (a t)")[:, 0:SCORES]
        sp = sqh[:, :, :].rearrange("p a t -> p (a t)")[:, 0:SCORES]
        sp_hi, sp_lo = (g[:, FC - 2:FC, :].rearrange("p a t -> p (a t)")[:, 0:SCORES] for g in (gh, gl))
        pa = xg[:, 0, :, :].rearrange("p a t -> p (a t)")[:, 0:SCORES]
        bank = ctx.enter_context(nc.psum_tensor("bank", [P, 8, 512], F32))

        cos, sin = table[:, C_COS:C_COS + T], table[:, C_SIN:C_SIN + T]
        ones, ident = (square[:, c:c + P] for c in (C_ONES, C_IDENT))
        ones_r, ident_r, neg_r, cum_r, allneg_r = (square_r[:, c:c + P] for c in (C_ONES, C_IDENT, C_NEG, C_CUM, C_ALL))

        bank67 = bank[:, 6:8, :].rearrange("p b c -> p (b c)")

        def strided_pair(c, step, n):
            return bank67[:, c:c + 2 * step].rearrange("p (i q) -> p i q", i=2)[:, :, 0:n]

        def twice(ap, q0):
            return ap[:, q0:T].unsqueeze(1).to_broadcast([P, 2, T - q0])

        def pair(n, q0):
            return bank[:, n:n + 2, q0:T]

        def first_query(l):
            return N_META if isinstance(l, int) and l == DEPTH - 1 else 0

        def rotary(k, qf):
            return (rq[:, 2 * k:2 * k + 2, qf:T], qf) if k < U_K else (rk[:, 2 * (k - U_K):2 * (k - U_K) + 2, 0:T], 0)

        def evicted(l, u):
            return l * UNITS + (u - U_V + 1)

        def layers(eng, layer):
            with eng.Fori(0, DEPTH - 1) as l:
                layer(l)
            layer(DEPTH - 1)

        raw_ready = [sem(f"raw_ready{i}") for i in range(RING)]
        hi_ready, lo_ready, piece_done = sem("hi_ready"), sem("lo_ready"), sem("piece_done")
        gains_in, gn_gains_in, table_in, squares_in = sem("gains_in"), sem("gn_gains_in"), sem("table_in"), sem("squares_in")
        h_loaded = [sem(f"h_loaded{p}") for p in range(PAIRS)]
        pads_ready, masks_ready, out_stored = sem("pads_ready"), sem("masks_ready"), sem("out_stored")
        scaled_out, out_ready, last_out = sem("scaled_out"), sem("out_ready"), sem("last_out")
        h_new, x_scaled, xh_ready, x_ready = sem("h_new"), sem("x_scaled"), sem("xh_ready"), sem("x_ready")
        sq_ready, ssq_added, ssum_done = sem("sq_ready"), sem("ssq_added"), sem("ssum_done")
        ms_ready, rms_ready, r_ready = sem("ms_ready"), sem("rms_ready"), sem("r_ready")
        gate_scaled, gate_act, up_gated = sem("gate_scaled"), sem("gate_act"), sem("up_gated")
        g_val, gh_ready, g_ready = sem("g_val"), sem("gh_ready"), sem("g_ready")
        unit_evicted, swapped, rot_cos, rot_sin, rotated = sem("unit_evicted"), sem("swapped"), sem("rot_cos"), sem("rot_sin"), sem("rotated")
        r_rotary, v_summed = sem("r_rotary"), sem("v_summed")
        v_turned, v_ready, rg_ready, sig_ready = sem("v_turned"), sem("v_ready"), sem("rg_ready"), sem("sig_ready")
        ret_scores, ret_decayed, ret_o, ro_ready = sem("ret_scores"), sem("ret_decayed"), sem("ret_o"), sem("ro_ready")
        rs_ready, rs_split, ret_var = sem("rs_ready"), sem("rs_split"), sem("ret_var")
        ln_ready, rr_ready, rn_ready, gated, rh_ready, ret_ready = (sem("ln_ready"), sem("rr_ready"), sem("rn_ready"),
                                                                  sem("gated"), sem("rh_ready"), sem("ret_ready"))
        z_done, sa_step, sp_made, sp_ready = sem("z_done"), sem("sa_step"), sem("sp_made"), sem("sp_ready")
        cum_done, pa_ready = sem("cum_done"), sem("pa_ready")
        sbo_done, sbh_ready, sb_ready = sem("sbo_done"), sem("sbh_ready"), sem("sb_ready")
        y_merged, yh_ready, y_ready = sem("y_merged"), sem("yh_ready"), sem("y_ready")

        block = ctx.enter_context(nc.Block())

        @block.sync
        def _(sp_):
            def load(j, n):
                sp_.dma_start(raw[:, j, :], stream[n]).then_inc(raw_ready[j], 16)

            def load_h(p):
                sp_.dma_start(h[:, 2 * p:2 * p + 2, :], h_in[:, 2 * p:2 * p + 2, :]).then_inc(h_loaded[p], 16)

            load(0, 0)
            load_h(1)
            load(1, 1)
            load_h(3)
            load(2, 2)
            load(3, 3)
            sp_.dma_start(square[:, :], squares[:, 0:C_NEG]).then_inc(squares_in, 16)
            sp_.dma_start(dec[:, 0:SQUARES - C_NEG], squares[:, C_NEG:SQUARES]).then_inc(squares_in, 16)
            for j in range(RING):
                sp_.wait_ge(lo_ready, j + 1)
                load(j, RING + j)
            sp_.dma_start(table[:, :], tables).then_inc(table_in, 16)
            sp_.dma_start(gn_gain[:, :, :], gn_gains).then_inc(gn_gains_in, 16)
            with sp_.Fori(2, DEPTH * PER_LAYER // RING) as i:
                for j in range(RING):
                    sp_.wait_ge(lo_ready, i * RING + (j - RING + 1))
                    load(j, i * RING + j)
            for p in (0, 1, 3, 2):
                if p < PAIRS - 1:
                    sp_.wait_ge(out_ready, p + 1)
                else:
                    sp_.wait_ge(last_out, 1)
                sp_.dma_start(h_out[:, 2 * p:2 * p + 2, :], h[:, 2 * p:2 * p + 2, N_META:T]).then_inc(out_stored, 16)
            sp_.wait_ge(out_stored, 16 * PAIRS)

        @block.gpsimd
        def _(pool):
            pool.memset(sk[:, :, T:PADT], 0.0).then_inc(pads_ready, 1)
            pool.memset(eps[:, :], EPS).then_inc(pads_ready, 1)

            def add_squares(rnd, p):
                pool.wait_ge(sq_ready, rnd * PAIRS + (p + 1))
                if p > 1:
                    pool.wait_ge(ssq_added, rnd * ADDS + (p - 1))
                pool.tensor_tensor(ssq[:, :, :], ssq[:, :, :], sqh[:, :, :], ALU.add).then_inc(ssq_added, 1)

            with pool.Fori(0, 3 * DEPTH) as rnd:
                for p in range(1, PAIRS):
                    add_squares(rnd, p)
            for p in range(1, PAIRS - 1):
                add_squares(3 * DEPTH, p)
            pool.wait_ge(r_ready, 3 * DEPTH + 1)
            pool.wait_ge(scaled_out, DC)
            pool.tensor_tensor(h[:, DC - 2:DC, N_META:T], h[:, DC - 2:DC, N_META:T], twice(r, N_META),
                               ALU.mult).then_inc(last_out, 1)

        @block.scalar
        def _(eng):
            def raw_count(n, slot):
                return (n - slot) * (16 // RING) + 16

            def split_hi(n, slot, first=False):
                if not first:
                    eng.wait_ge(piece_done, n - (RING - 1))
                eng.wait_ge(raw_ready[slot], raw_count(n, slot))
                eng.activation(w_hi[:, slot, :], raw[:, slot, :], ACT.Copy).then_inc(hi_ready, 1)

            def hi_of_h(rnd, p, q0):
                c = 2 * p
                eng.wait_ge(x_scaled, rnd * DC + (c + 2))
                eng.activation(xh[:, c:c + 2, q0:T], xg[:, p % 2, :, q0:T], ACT.Copy).then_inc(xh_ready, 1)

            def squares_of_h(rnd, p, q0):
                c = 2 * p
                if p == 0:
                    eng.activation(ssq[:, :, q0:T], h[:, 0:2, q0:T], ACT.Square).then_inc(sq_ready, 1)
                else:
                    if p > 1:
                        eng.wait_ge(ssq_added, rnd * ADDS + (p - 1))
                    eng.activation(sqh[:, :, q0:T], h[:, c:c + 2, q0:T], ACT.Square).then_inc(sq_ready, 1)

            def take_h(rnd, p, q0, final=False):
                eng.wait_ge(h_new, (rnd - 1) * PAIRS + (p + 1))
                if not final:
                    hi_of_h(rnd, p, q0)
                squares_of_h(rnd, p, q0)

            def rms(rnd, q0):
                eng.wait_ge(ms_ready, rnd + 1)
                eng.activation(r[:, q0:T], ms[:, q0:T], ACT.Sqrt).then_inc(rms_ready, 1)

            def ffn(l, f):
                fi = l * 2 + f
                off = 0 if f == 0 else FFN + MIX
                base = l * PER_LAYER + off
                last = first_query(l) > 0 and f == 1
                q0 = first_query(l) if f else 0
                rms(l * 3 + 2 * f, q0)
                eng.preload_act_table_set("silu_and_others")
                with eng.Fori(0, ITERS) as it:
                    for j in range(4):
                        split_hi(base + it * 4 + (j + RING), (off + j) % RING)
                        if j == 1:
                            eng.wait_ge(gate_scaled, fi * ITERS + it + 1)
                            eng.activation(act[:, :, q0:T], scl[:, :, q0:T], ACT.Silu).then_inc(gate_act, 1)
                    eng.wait_ge(g_val, fi * ITERS + it + 1)
                    eng.activation(gh[:, bass.ds(it * 2, 2), q0:T], gv[:, :, q0:T], ACT.Copy).then_inc(gh_ready, 1)
                eng.preload_act_table_set("sqrt_and_others")
                for q in range(QUADS):
                    for c in range(ITERS):
                        s = GU + q * ITERS + c
                        if c >= ITERS - 2:
                            take_h(l * 3 + 2 * f + 1, 2 * q + c - (ITERS - 2), q0, final=last)
                        if not last or s + RING < FFN:
                            split_hi(base + (s + RING), (off + s) % RING)

            def mixer(l):
                base = l * PER_LAYER + FFN
                qf = first_query(l)
                for s in range(MIX):
                    if s >= S_OUT and s % 2:
                        take_h(l * 3 + 2, (s - S_OUT) // 2, qf)
                    split_hi(base + (s + RING), (FFN + s) % RING)
                    u = s // 2
                    if s == 1:
                        rms(l * 3 + 1, 0)
                    if s == 2 * U_V:
                        eng.preload_act_table_set("silu_and_others")
                    if s % 2 and u < U_V:
                        q0 = rotary(u, qf)[1]
                        if u:
                            eng.wait_ge(rotated, l * U_V + u)
                        for q in range(4):
                            a, b = 32 * q, 32 * (q ^ 1)
                            eng.activation(act[b:b + 32, :, q0:T], bank[a:a + 32, 2 * (u % 2):2 * (u % 2) + 2, q0:T],
                                           ACT.Copy).then_inc(swapped, 1)
                    k = s // 2 - 1 - U_SV
                    if s % 2 == 0 and 0 <= k < 2:
                        eng.wait_ge(v_turned, l * 6 + (4 + k + 1))
                        eng.activation(sv[:, 0:2, 256 * k:256 * k + 256],
                                       bank[:, 6, :].rearrange("p (i f) -> p i f", i=2), ACT.Copy).then_inc(v_ready, 1)
                        eng.activation(sv[0:TOK[2][1], 2, 256 * k:256 * k + 256],
                                       bank[0:TOK[2][1], 7, 0:256], ACT.Copy).then_inc(v_ready, 1)
                    if s % 2 and U_G <= u < U_SQ:
                        eng.wait_ge(unit_evicted, evicted(l, u))
                        c = 2 * (u - U_G)
                        eng.activation(rg[:, c:c + 2, qf:T], scl[:, :, qf:T], ACT.Silu).then_inc(rg_ready, 1)
                    if s == RET0:
                        eng.preload_act_table_set("natural_log_exp_and_others")
                    hd = (s - RET0 - 3) // 2
                    if (s - RET0) % 2 == 1 and 0 <= hd < HEADS:
                        eng.wait_ge(gated, l * HEADS + (hd + 1))
                        eng.activation(gh[:, RET_C + hd, qf:T], rn[:, qf:T], ACT.Copy).then_inc(rh_ready, 1)
                    hd = (s - RET0 - 1) // 2
                    if (s - RET0) % 2 == 1 and 0 <= hd < HEADS:
                        eng.wait_ge(ret_o, l * HEADS + (hd + 1))
                        eng.activation(ro[:, qf:T], bank[:, 5, qf:T], ACT.Copy).then_inc(ro_ready, 1)
                        eng.activation(rs[:, qf:T], bank[:, 5, qf:T], ACT.Square).then_inc(rs_ready, 1)
                        eng.activation(rs_hi[:, qf:T], bank[:, 5, qf:T], ACT.Square).then_inc(rs_ready, 1)
                    hd = (s - RET0 - 2) // 2
                    if (s - RET0) % 2 == 0 and 0 <= hd < HEADS:
                        eng.wait_ge(ret_var, l * HEADS + (hd + 1))
                        eng.activation(rr[:, qf:T], bank[:, 5, qf:T], ACT.Ln, bias=eps[:, 0:1]).then_inc(ln_ready, 1)
                        eng.wait_ge(ln_ready, l * HEADS + (hd + 1))
                        eng.activation(rr[:, qf:T], rr[:, qf:T], ACT.Exp, scale=-0.5).then_inc(rr_ready, 1)
                    hd = (s - SB0) // 2
                    if (s - SB0) % 2 == 0 and 0 <= hd < HEADS:
                        eng.wait_ge(z_done, l * HEADS + (hd + 1))
                        eng.activation(sa[:, qf:], bank[:, 6, qf:SCORES], ACT.Abs).then_inc(sa_step, 1)
                        eng.wait_ge(sa_step, l * 3 * HEADS + (3 * hd + 1))
                        eng.activation(sa[:, qf:], sa[:, qf:], ACT.Exp, scale=-1.0).then_inc(sa_step, 1)
                        eng.wait_ge(sa_step, l * 3 * HEADS + (3 * hd + 2))
                        eng.activation(sa[:, qf:], sa[:, qf:], ACT.Ln, bias=1.0).then_inc(sa_step, 1)
                    hd = (s - SB0 - 3) // 2
                    if (s - SB0) % 2 == 1 and 0 <= hd < HEADS and hd % 2:
                        eng.wait_ge(sbo_done, l * HEADS + (hd + 1))
                        eng.activation(gh[:, SB_C + hd // 2, qf:T], bank[:, 7, qf:T], ACT.Copy).then_inc(sbh_ready, 1)
                    hd = (s - SB0 - 1) // 2
                    if (s - SB0) % 2 == 1 and 0 <= hd < HEADS:
                        eng.wait_ge(cum_done, l * HEADS + (hd + 1))
                        eng.activation(pa[:, qf:], bank[:, 6, qf:SCORES], ACT.Exp).then_inc(pa_ready, 1)
                    k = s - (SB0 + 2 * HEADS)
                    if 0 <= k < PAIRS:
                        for gate, u0 in ((ga, U_GA), (gb, U_GB)):
                            eng.wait_ge(unit_evicted, evicted(l, u0 + k))
                            eng.activation(gate[:, 2 * k:2 * k + 2, qf:T], gate[:, 2 * k:2 * k + 2, qf:T],
                                           ACT.Sigmoid).then_inc(sig_ready, 1)
                    if S_Y <= s < S_OUT and Y_STEPS[s - S_Y][1] == "s":
                        k = Y_STEPS[s - S_Y][2]
                        eng.wait_ge(y_merged, l * PAIRS + (k + 1))
                        c = MERGE_C + 2 * k
                        eng.activation(gh[:, c:c + 2, qf:T], ga[:, 2 * k:2 * k + 2, qf:T], ACT.Copy).then_inc(yh_ready, 1)
                    if s == S_OUT - 1:
                        eng.preload_act_table_set("sqrt_and_others")

            def layer(l):
                ffn(l, 0)
                mixer(l)
                ffn(l, 1)

            eng.dma_start(h[:, 0:2, :], h_in[:, 0:2, :]).then_inc(h_loaded[0], 16)
            eng.dma_start(gain[:, :, :], gains).then_inc(gains_in, 16)
            eng.preload_act_table_set("sqrt_and_others")
            eng.dma_start(h[:, 4:6, :], h_in[:, 4:6, :]).then_inc(h_loaded[2], 16)
            for j, pairs in enumerate([[0], [1], [2, 3], []]):
                split_hi(j, j, first=True)
                for p in pairs:
                    hi_of_h(0, p, 0)
                    eng.wait_ge(h_loaded[p], 16)
                    squares_of_h(0, p, 0)
            eng.wait_ge(pads_ready, 2)
            layers(eng, layer)
            rms(3 * DEPTH, N_META)

        @block.vector
        def _(eng):
            def split_lo(n, slot):
                eng.wait_ge(hi_ready, n + 1)
                eng.tensor_tensor(w_lo[:, slot, :], raw[:, slot, :], w_hi[:, slot, :].bitcast(F32),
                                  ALU.subtract).then_inc(lo_ready, 1)

            def scale_h(rnd, p, q0):
                if not (isinstance(rnd, int) and rnd == 0 and p < 2):
                    eng.wait_ge(x_ready, rnd * PAIRS + (p - 1))
                for c in range(2):
                    eng.tensor_scalar(xg[:, p % 2, c, q0:T], h[:, 2 * p + c, q0:T], gain[:, bass.ds(rnd, 1), 2 * p + c],
                                      None, ALU.mult).then_inc(x_scaled, 1)

            def lo_of_h(rnd, p, q0):
                c = 2 * p
                eng.wait_ge(xh_ready, rnd * PAIRS + (p + 1))
                eng.tensor_tensor(xl[:, c:c + 2, q0:T], xg[:, p % 2, :, q0:T], xh[:, c:c + 2, q0:T].bitcast(F32),
                                  ALU.subtract).then_inc(x_ready, 1)

            def norm_factor(rnd, q0):
                eng.wait_ge(ssum_done, rnd + 1)
                eng.tensor_scalar(ms[:, q0:T], bank[:, 4, q0:T], 1.0 / DC, EPS, ALU.mult, ALU.add).then_inc(ms_ready, 1)
                eng.wait_ge(rms_ready, rnd + 1)
                eng.reciprocal(r[:, q0:T], r[:, q0:T]).then_inc(r_ready, 1)

            def update_h(rnd, p, b, factor, q0, final=False):
                c = 2 * p
                eng.scalar_tensor_tensor(h[:, c:c + 2, q0:T], pair(b, q0), factor, h[:, c:c + 2, q0:T],
                                         ALU.mult, ALU.add).then_inc(h_new, 1)
                if final:
                    eng.wait_ge(sq_ready, rnd * PAIRS + (p + 1))
                    for k in (c, c + 1):
                        eng.tensor_scalar(h[:, k, q0:T], h[:, k, q0:T], gain[:, rnd, k:k + 1], None,
                                          ALU.mult).then_inc(scaled_out, 1)
                else:
                    eng.wait_ge(h_new, (rnd - 1) * PAIRS + (p + 1))
                    scale_h(rnd, p, q0)
                    lo_of_h(rnd, p, q0)

            def ffn(l, f):
                fi = l * 2 + f
                off = 0 if f == 0 else FFN + MIX
                base = l * PER_LAYER + off
                last = first_query(l) > 0 and f == 1
                q0 = first_query(l) if f else 0
                norm_factor(l * 3 + 2 * f, q0)
                with eng.Fori(0, ITERS) as it:
                    i = fi * ITERS + it
                    for j in range(4):
                        if j == 1:
                            eng.wait_ge(r_ready, l * 3 + 2 * f + 1)
                            eng.wait_ge(piece_done, base + it * 4 + 2)
                            eng.tensor_tensor(scl[:, :, q0:T], pair(0, q0), twice(r, q0), ALU.mult).then_inc(gate_scaled, 1)
                        if j == 3:
                            eng.wait_ge(gate_act, i + 1)
                            eng.wait_ge(g_ready, i + 1)
                            eng.wait_ge(piece_done, base + it * 4 + 4)
                            eng.tensor_tensor(gv[:, :, q0:T], pair(2, q0), act[:, :, q0:T], ALU.mult).then_inc(up_gated, 1)
                        split_lo(base + it * 4 + (j + RING), (off + j) % RING)
                    eng.wait_ge(up_gated, i + 1)
                    eng.tensor_tensor(gv[:, :, q0:T], gv[:, :, q0:T], twice(r, q0), ALU.mult).then_inc(g_val, 1)
                    eng.wait_ge(gh_ready, i + 1)
                    eng.tensor_tensor(gl[:, bass.ds(it * 2, 2), q0:T], gv[:, :, q0:T],
                                      gh[:, bass.ds(it * 2, 2), q0:T].bitcast(F32), ALU.subtract).then_inc(g_ready, 1)
                for q in range(QUADS):
                    for c in range(ITERS):
                        s = GU + q * ITERS + c
                        if c >= ITERS - 2:
                            k = c - (ITERS - 2)
                            eng.wait_ge(piece_done, base + (s + 1))
                            update_h(l * 3 + 2 * f + 1, 2 * q + k, 4 * q + 2 * k, 0.5, q0, final=last)
                        for n in [] if s == FFN - 2 else [s - 1, s] if s == FFN - 1 else [s]:
                            if not last or n + RING < FFN:
                                split_lo(base + (n + RING), (off + n) % RING)

            def mixer(l):
                base = l * PER_LAYER + FFN
                qf = first_query(l)
                eng.wait_ge(table_in, 16)
                eng.wait_ge(gn_gains_in, 16)
                for s in range(MIX):
                    u = s // 2
                    if s == 1:
                        norm_factor(l * 3 + 1, 0)
                        eng.wait_ge(r_ready, l * 3 + 2)
                        eng.tensor_tensor(r_cos, cos, r[:, :], ALU.mult).then_inc(r_rotary, 1)
                        eng.tensor_tensor(r_sin, sin, r[:, :], ALU.mult).then_inc(r_rotary, 1)
                        eng.wait_ge(r_rotary, 2 * l + 2)
                    if s % 2 == 0 and 0 < u <= U_V:
                        k = u - 1
                        dst, q0 = rotary(k, qf)
                        eng.tensor_tensor(act[:, :, q0:T], act[:, :, q0:T], twice(r_sin, q0), ALU.mult).then_inc(rot_sin, 1)
                        eng.wait_ge(rot_sin, l * U_V + (k + 1))
                        eng.wait_ge(rot_cos, l * U_V + (k + 1))
                        eng.tensor_tensor(dst, dst, act[:, :, q0:T], ALU.add).then_inc(rotated, 1)
                    hd = (s - RET0 - 3) // 2
                    if (s - RET0) % 2 == 1 and 0 <= hd < HEADS:
                        eng.wait_ge(rr_ready, l * HEADS + (hd + 1))
                        if hd:
                            eng.wait_ge(ret_ready, l * HEADS + hd)
                        eng.tensor_tensor(rn[:, qf:T], ro[:, qf:T], rr[:, qf:T], ALU.mult).then_inc(rn_ready, 1)
                        eng.wait_ge(rn_ready, l * HEADS + (hd + 1))
                        eng.wait_ge(rg_ready, l * PAIRS + (hd // 2 + 1))
                        eng.scalar_tensor_tensor(rn[:, qf:T], rn[:, qf:T], gn_gain[:, bass.ds(l, 1), hd], rg[:, hd, qf:T],
                                                 ALU.mult, ALU.mult).then_inc(gated, 1)
                    hd = (s - RET0 - 4) // 2
                    if (s - RET0) % 2 == 0 and 0 <= hd < HEADS:
                        eng.wait_ge(rh_ready, l * HEADS + (hd + 1))
                        eng.tensor_tensor(gl[:, RET_C + hd, qf:T], rn[:, qf:T], gh[:, RET_C + hd, qf:T].bitcast(F32),
                                          ALU.subtract).then_inc(ret_ready, 1)
                    hd = (s - RET0 - 2) // 2
                    if (s - RET0) % 2 == 0 and 0 <= hd < HEADS:
                        eng.wait_ge(rs_ready, l * 2 * HEADS + 2 * (hd + 1))
                        eng.tensor_tensor(rs_lo[:, qf:T], rs[:, qf:T], rs_hi[:, qf:T].bitcast(F32), ALU.subtract).then_inc(rs_split, 1)
                    hd = (s - SB0 - 1) // 2
                    if (s - SB0) % 2 == 1 and 0 <= hd < HEADS:
                        eng.wait_ge(sa_step, l * 3 * HEADS + 3 * (hd + 1))
                        for whole_or_hi in (sp, sp_hi):
                            eng.scalar_tensor_tensor(whole_or_hi[:, qf:], bank[:, 6, qf:SCORES], 0.0, sa[:, qf:],
                                                     ALU.max, ALU.add).then_inc(sp_made, 1)
                        eng.wait_ge(sp_made, l * 2 * HEADS + 2 * (hd + 1))
                        eng.tensor_tensor(sp_lo[:, qf:], sp[:, qf:], sp_hi[:, qf:].bitcast(F32), ALU.subtract).then_inc(sp_ready, 1)
                    hd = (s - SB0 - 4) // 2
                    if (s - SB0) % 2 == 0 and 0 <= hd < HEADS and hd % 2:
                        eng.wait_ge(sbh_ready, l * PAIRS + (hd // 2 + 1))
                        c = SB_C + hd // 2
                        eng.tensor_tensor(gl[:, c, qf:T], bank[:, 7, qf:T], gh[:, c, qf:T].bitcast(F32),
                                          ALU.subtract).then_inc(sb_ready, 1)
                    if S_Y < s < S_OUT:
                        j, kind, k, half = Y_STEPS[s - S_Y - 1]
                        if kind == "r" and half:
                            eng.wait_ge(sig_ready, l * 2 * PAIRS + (2 * k + 2))
                            c = 2 * k
                            eng.tensor_tensor(ga[:, c:c + 2, qf:T], pair(Y_BANKS[j % 3], qf), ga[:, c:c + 2, qf:T],
                                              ALU.mult).then_inc(unit_evicted, 1)

                    def merged_lo(k):
                        c = MERGE_C + 2 * k
                        eng.wait_ge(yh_ready, l * PAIRS + (k + 1))
                        eng.tensor_tensor(gl[:, c:c + 2, qf:T], ga[:, 2 * k:2 * k + 2, qf:T],
                                          gh[:, c:c + 2, qf:T].bitcast(F32), ALU.subtract).then_inc(y_ready, 1)

                    if S_Y < s < S_OUT and Y_STEPS[s - S_Y - 1][1] == "s":
                        merged_lo(Y_STEPS[s - S_Y - 1][2])

                    eng.wait_ge(piece_done, base + (s + 1))
                    if s % 2 and u < U_Y:
                        q0 = 0 if U_K <= u < U_G or U_SK <= u < U_GA else qf
                        res, rb = pair(2 * (u % 2), q0), twice(r, q0)
                        if u < U_V:
                            eng.wait_ge(swapped, l * 4 * U_V + 4 * (u + 1))
                            eng.tensor_tensor(rotary(u, qf)[0], res, twice(r_cos, q0), ALU.mult).then_inc(rot_cos, 1)
                        elif u < U_SQ or U_SV <= u < U_GA:
                            if u == U_V:
                                eng.wait_ge(rot_sin, l * U_V + U_V)
                            if U_V < u <= U_G:
                                eng.wait_ge(v_turned, l * 6 + (u - U_V))
                            if U_G < u < U_SQ:
                                eng.wait_ge(rg_ready, l * PAIRS + (u - U_G))
                            if u == U_SV:
                                eng.wait_ge(rg_ready, l * PAIRS + PAIRS)
                            if u == U_SV + 1:
                                eng.wait_ge(v_turned, l * 6 + 5)
                            eng.tensor_tensor(scl[:, :, q0:T], res, rb, ALU.mult).then_inc(unit_evicted, 1)
                        elif u < U_SK:
                            c = 2 * (u - U_SQ)
                            eng.scalar_tensor_tensor(sq[:, c:c + 2, q0:T], res, DK ** -0.5, rb,
                                                     ALU.mult, ALU.mult).then_inc(unit_evicted, 1)
                        else:
                            dst, u0 = (sk, U_SK) if u < U_SV else (ga, U_GA) if u < U_GB else (gb, U_GB)
                            c = 2 * (u - u0)
                            eng.tensor_tensor(dst[:, c:c + 2, q0:T], res, rb, ALU.mult).then_inc(unit_evicted, 1)
                    if S_Y <= s < S_OUT and Y_STEPS[s - S_Y][1] == "s":
                        j, _, k, _ = Y_STEPS[s - S_Y]
                        c = 2 * k
                        eng.wait_ge(sig_ready, l * 2 * PAIRS + (2 * k + 2))
                        eng.tensor_tensor(gb[:, c:c + 2, qf:T], pair(Y_BANKS[j % 3], qf), gb[:, c:c + 2, qf:T],
                                          ALU.mult).then_inc(unit_evicted, 1)
                        eng.wait_ge(unit_evicted, evicted(l, U_Y + j))
                        eng.tensor_tensor(ga[:, c:c + 2, qf:T], ga[:, c:c + 2, qf:T], gb[:, c:c + 2, qf:T],
                                          ALU.add).then_inc(y_merged, 1)
                        if s == S_OUT - 1:
                            merged_lo(k)
                    if s >= S_OUT and s % 2:
                        p = (s - S_OUT) // 2
                        update_h(l * 3 + 2, p, OUT_BANKS[p], 1.0, qf)
                    for n in [] if s == MIX - 2 else [s - 1, s] if s == MIX - 1 else [s]:
                        split_lo(base + (n + RING), (FFN + n) % RING)
                    k = s // 2 - 1 - U_V
                    if s % 2 == 0 and 0 <= k < 4:
                        n = TOK[2][1]
                        turned = bank[:, 4, :].rearrange("p (i m f) -> p i m f", i=2, m=2)
                        turned2 = bank[0:n, 5, 0:2 * P].rearrange("p (m f) -> p m f", m=2)
                        eng.wait_ge(v_turned, l * 6 + (k + 1))
                        if k:
                            eng.wait_ge(v_ready, l * 12 + 2 * k)
                        eng.tensor_reduce(vsum[:, 0:2, :], turned, mybir.AxisListType.X, ALU.add).then_inc(v_summed, 1)
                        eng.tensor_reduce(vsum[0:n, 2, :], turned2, mybir.AxisListType.X, ALU.add).then_inc(v_summed, 1)
                        eng.wait_ge(v_summed, l * 8 + 2 * (k + 1))
                        eng.scalar_tensor_tensor(rv[:, 0:2, 256 * k:256 * k + 256].rearrange("p i (m f) -> p i m f", m=2),
                                                 vsum[:, 0:2, :].unsqueeze(3).to_broadcast([P, 2, 2, P]), -1.0 / DV, turned,
                                                 ALU.mult, ALU.add).then_inc(v_ready, 1)
                        eng.scalar_tensor_tensor(rv[0:n, 2, 256 * k:256 * k + 256].rearrange("p (m f) -> p m f", m=2),
                                                 vsum[0:n, 2, :].unsqueeze(2).to_broadcast([n, 2, P]), -1.0 / DV, turned2,
                                                 ALU.mult, ALU.add).then_inc(v_ready, 1)
                    hd = (s - RET0) // 2
                    if (s - RET0) % 2 == 0 and 0 <= hd < HEADS:
                        c = C_DECAY + hd * SCORES
                        if hd:
                            eng.wait_ge(ret_o, l * HEADS + hd)
                        eng.wait_ge(ret_scores, l * HEADS + (hd + 1))
                        eng.tensor_tensor(dec[:, qf:], bank[:, 4, qf:SCORES], table[:, c + qf:c + SCORES],
                                          ALU.mult).then_inc(ret_decayed, 1)

            def layer(l):
                ffn(l, 0)
                mixer(l)
                ffn(l, 1)

            eng.memset(gv[:, :, :], 0.0).then_inc(g_ready, 1)
            eng.wait_ge(gains_in, 16)
            for p in range(PAIRS):
                eng.wait_ge(h_loaded[p], 16)
                scale_h(0, p, 0)
                if p == 0:
                    split_lo(0, 0)
                lo_of_h(0, p, 0)
                if p == 1:
                    split_lo(1, 1)
            split_lo(2, 2)
            split_lo(3, 3)
            eng.wait_ge(squares_in, 32)
            eng.tensor_copy(square_r[:, 0:C_NEG], square[:, :]).then_inc(masks_ready, 1)
            eng.tensor_copy(square_r[:, C_NEG:], dec[:, 0:SQUARES - C_NEG]).then_inc(masks_ready, 1)
            layers(eng, layer)
            norm_factor(3 * DEPTH, N_META)
            eng.wait_ge(r_ready, 3 * DEPTH + 1)
            eng.wait_ge(scaled_out, DC)
            for p in range(PAIRS - 1):
                eng.tensor_tensor(h[:, 2 * p:2 * p + 2, N_META:T], h[:, 2 * p:2 * p + 2, N_META:T], twice(r, N_META),
                                  ALU.mult).then_inc(out_ready, 1)

        @block.tensor
        def _(pe):
            def use(n, slot, blocks, before=None):
                pe.wait_ge(lo_ready, n + 1)
                for b, (hi, lo, out, first, last) in enumerate(blocks):
                    if before and b in before:
                        before[b]()
                    wh = w_hi[:, slot, b * P:(b + 1) * P]
                    wl = w_lo[:, slot, b * P:(b + 1) * P]
                    pe.matmul(out, wh, hi, start=first, stop=False)
                    pe.matmul(out, wh, lo, start=False, stop=False)
                    mm = pe.matmul(out, wl, hi, start=False, stop=last)
                mm.then_inc(piece_done, 1)

            def k_half(src_h, src_l, half, b, q0, halves=2, c0=0):
                return [(src_h[:, c0 + 4 * half + k, q0:T], src_l[:, c0 + 4 * half + k, q0:T], bank[:, b + m, q0:T],
                         half == 0 and k == 0, half == halves - 1 and k == 3) for k in range(4) for m in range(2)]

            def sum_of_squares(rnd, q0, final=False):
                pe.wait_ge(squares_in, 32)
                pe.wait_ge(ssq_added, rnd * ADDS + (ADDS - 1 if final else ADDS))
                pe.matmul(bank[:, 4, q0:T], ones, ssq[:, 0, q0:T], start=True, stop=False)
                mm = pe.matmul(bank[:, 4, q0:T], ones, ssq[:, 1, q0:T], start=False, stop=not final)
                if final:
                    pe.wait_ge(sq_ready, rnd * PAIRS + PAIRS)
                    pe.matmul(bank[:, 4, q0:T], ones, sqh[:, 0, q0:T], start=False, stop=False)
                    mm = pe.matmul(bank[:, 4, q0:T], ones, sqh[:, 1, q0:T], start=False, stop=True)
                mm.then_inc(ssum_done, 1)

            def first_unit(rnd, piece, q0, b):
                def wait_x(p):
                    pe.wait_ge(x_ready, rnd * PAIRS + (p + 1))

                wait_x(0)
                piece(0, {0: lambda: wait_x(2) if b else None, 4: lambda: wait_x(1)})
                piece(1, {0: lambda: wait_x(2), 4: lambda: wait_x(3)})

            def ffn(l, f):
                fi = l * 2 + f
                off = 0 if f == 0 else FFN + MIX
                base = l * PER_LAYER + off
                q0 = first_query(l) if f else 0

                def gate(n, half, before=None):
                    use(n, (off + half) % RING, k_half(xh, xl, half, 0, q0), before)

                def up(n, half, before=None):
                    use(n, (off + 2 + half) % RING, k_half(xh, xl, half, 2, q0), before)

                first_unit(l * 3 + 2 * f, lambda half, before: gate(base + half, half, before), q0, f)
                up(base + 2, 0, {2 if f else 0: lambda: sum_of_squares(l * 3 + 2 * f, q0)})
                up(base + 3, 1)
                with pe.Fori(1, ITERS) as it:
                    pe.wait_ge(gate_scaled, fi * ITERS + it)
                    gate(base + it * 4, 0)
                    gate(base + it * 4 + 1, 1)
                    pe.wait_ge(up_gated, fi * ITERS + it)
                    up(base + it * 4 + 2, 0)
                    up(base + it * 4 + 3, 1)
                pe.wait_ge(gate_scaled, fi * ITERS + ITERS)
                for q in range(QUADS):
                    for c in range(ITERS):
                        if q == 0 and c < ITERS - 1:
                            pe.wait_ge(g_ready, fi * ITERS + (c + 2 if c < ITERS - 2 else ITERS + 1))
                        if c < ITERS - 2:
                            blocks = [(2 * c + k, m, c == 0 and k == 0, False) for m in range(4) for k in range(2)]
                        else:
                            m0, k0 = 2 * (c - (ITERS - 2)), FC - 4
                            blocks = [(k0 + k, m0 + m, False, k == 3) for k in range(4) for m in range(2)]
                        s = GU + q * ITERS + c
                        use(base + s, (off + s) % RING,
                            [(gh[:, k, q0:T], gl[:, k, q0:T], bank[:, 4 * q + m, q0:T], first, last)
                             for k, m, first, last in blocks],
                            {4: lambda: pe.wait_ge(up_gated, fi * ITERS + ITERS)} if q == c == 0 else None)

            def turn_values(b):
                for m in range(2):
                    for j, (t0, n) in enumerate(TOK):
                        out = bank[0:n, b, 256 * j + P * m:256 * j + P * m + P] if j < 2 else bank[0:n, b + 1, P * m:P * m + P]
                        mm = pe.transpose(out, scl[:, m, t0:t0 + n], ident)
                mm.then_inc(v_turned, 1)

            def mixer(l):
                base = l * PER_LAYER + FFN
                rnd = l * 3 + 1
                qf = first_query(l)

                def piece(s, blocks, before=None):
                    use(base + s, (FFN + s) % RING, blocks, before)

                def subtract_sums(hd):
                    pe.wait_ge(sp_ready, l * HEADS + (hd + 1))
                    n = TOK[2][1]
                    for part in (sp_hi, sp_lo):
                        def add_sum(out, weights, summed):
                            return pe.matmul(out, weights, summed, start=False, stop=True, skip_group_check=True)

                        add_sum(bank[:, 6, qf:SCORES], cum_r, part[:, qf:])
                        add_sum(bank[:, 6, P:SEG[1]], allneg_r, part[:, SEG[1]:SEG[2]])
                        mm = add_sum(strided_pair(SEG[1] - n, T - P, n), allneg_r,
                                     part[:, SEG[2]:SCORES].unsqueeze(1).to_broadcast([P, 2, n]))
                    mm.then_inc(cum_done, 1)

                first_unit(rnd, lambda half, before: piece(half, k_half(xh, xl, half, 0, qf), before), 0, 0)
                for s in range(2, MIX):
                    u = s // 2
                    before = {}
                    if s == 2:
                        before[0] = lambda: sum_of_squares(rnd, 0)
                    hd = (s - SB0 - 2) // 2
                    if (s - SB0) % 2 == 0 and 0 <= hd < HEADS:
                        before[3] = lambda hd=hd: subtract_sums(hd)
                    if s < S_Y:
                        if s % 2 == 0 and 2 <= u < U_V + 2:
                            pe.wait_ge(rot_cos, l * U_V + (u - 1))
                        elif s % 2 == 0 and u >= 2:
                            pe.wait_ge(unit_evicted, evicted(l, u - 2))
                        q0 = 0 if U_K <= u < U_G or U_SK <= u < U_GA else qf
                        piece(s, k_half(xh, xl, s % 2, 2 * (u % 2), q0), before)
                    elif s < S_OUT:
                        j, kind, k, half = Y_STEPS[s - S_Y]
                        if s == S_Y:
                            pe.wait_ge(ret_ready, l * HEADS + HEADS)
                        if half == 0 and j != 2:
                            pe.wait_ge(unit_evicted, evicted(l, U_Y + j - (2 if j < 2 else 3)))
                        if (kind, k) == ("s", 0):
                            pe.wait_ge(sb_ready, l * PAIRS + PAIRS)
                        if kind == "r":
                            piece(s, k_half(gh, gl, half, Y_BANKS[j % 3], qf, c0=RET_C), before)
                        else:
                            piece(s, k_half(gh, gl, 0, Y_BANKS[j % 3], qf, halves=1, c0=SB_C), before)
                    else:
                        p, half = (s - S_OUT) // 2, s % 2
                        if half == 0 and p:
                            pe.wait_ge(unit_evicted, evicted(l, U_Y + OUT_AFTER[p]))
                        blocks = k_half(gh, gl, half, OUT_BANKS[p], qf, c0=MERGE_C)
                        if p == 0:
                            piece(s, blocks, {0: lambda: pe.wait_ge(y_ready, l * PAIRS + (2 * half + 1)),
                                              4: lambda: pe.wait_ge(y_ready, l * PAIRS + (2 * half + 2))})
                        else:
                            piece(s, blocks)
                    for u0, cnt, first, b in ((U_V, 4, 0, 4), (U_SV, 2, 4, 6)):
                        k = s // 2 - 1 - u0
                        if s % 2 == 0 and 0 <= k < cnt:
                            if s == 2 * U_V + 2:
                                pe.wait_ge(squares_in, 32)
                            pe.wait_ge(unit_evicted, evicted(l, u0 + k))
                            if k:
                                pe.wait_ge(v_ready, l * 12 + 2 * (first + k))
                            turn_values(b)
                    hd = (s - RET0 - 1) // 2
                    if (s - RET0) % 2 == 1 and 0 <= hd < HEADS:
                        pe.wait_ge(ret_decayed, l * HEADS + (hd + 1))
                        if hd:
                            pe.wait_ge(ln_ready, l * HEADS + hd)
                        for i, (t0, cnt) in enumerate(TOK):
                            q = max(t0, qf)
                            c = SEG[i] + q - t0
                            mm = pe.matmul(bank[:, 5, q:T], rv[0:cnt, i, hd * DV:(hd + 1) * DV],
                                           dec[0:cnt, c:c + T - q], start=(i == 0), stop=(i == 2))
                        mm.then_inc(ret_o, 1)
                    hd = (s - RET0 - 2) // 2
                    if (s - RET0) % 2 == 0 and 0 <= hd < HEADS:
                        pe.wait_ge(rs_split, l * HEADS + (hd + 1))
                        pe.matmul(bank[:, 5, qf:T], ones_r, rs_hi[:, qf:T], start=True, stop=False)
                        pe.matmul(bank[:, 5, qf:T], ones_r, rs_lo[:, qf:T], start=False, stop=True).then_inc(ret_var, 1)
                    hd = (s - RET0) // 2
                    if (s - RET0) % 2 == 0 and 0 <= hd < HEADS:
                        if hd == 0:
                            pe.wait_ge(pads_ready, 2)
                            pe.wait_ge(masks_ready, 2)
                            pe.wait_ge(rotated, l * U_V + U_V)
                            pe.wait_ge(v_ready, l * 12 + 8)
                        f0 = DK * (hd % 2)
                        for i, (t0, cnt) in enumerate(TOK):
                            q = max(t0, qf)
                            c = SEG[i] + q - t0
                            mm = pe.matmul(bank[0:cnt, 4, c:c + T - q], rk[f0:f0 + DK, hd // 2, t0:t0 + cnt],
                                           rq[f0:f0 + DK, hd // 2, q:T], start=(i == 0), stop=True, skip_group_check=True)
                        mm.then_inc(ret_scores, 1)
                    hd = (s - SB0 - 3) // 2
                    if (s - SB0) % 2 == 1 and 0 <= hd < HEADS:
                        pe.wait_ge(pa_ready, l * HEADS + (hd + 1))
                        if hd >= 2 and hd % 2 == 0:
                            pe.wait_ge(sb_ready, l * PAIRS + hd // 2)
                        f0 = DK * (hd % 2)
                        for i, (t0, cnt) in enumerate(TOK):
                            q = max(t0, qf)
                            c = SEG[i] + q - t0
                            mm = pe.matmul(bank[f0:f0 + DK, 7, q:T], sv[0:cnt, i, hd * DK:(hd + 1) * DK],
                                           pa[0:cnt, c:c + T - q], start=(i == 0), stop=(i == 2))
                        mm.then_inc(sbo_done, 1)
                    hd = (s - SB0) // 2
                    if (s - SB0) % 2 == 0 and 0 <= hd < HEADS:
                        if hd == 0:
                            pe.wait_ge(v_ready, l * 12 + 12)
                        else:
                            pe.wait_ge(pa_ready, l * HEADS + hd)
                        f0 = DK * (hd % 2)
                        for i, (t0, cnt) in enumerate(TOK):
                            q = max(t0, qf)
                            c = SEG[i] + q - t0
                            pe.matmul(bank[:, 6, c:c + T - q], sk[f0:f0 + DK, hd // 2, t0:t0 + P],
                                      sq[f0:f0 + DK, hd // 2, q:T], start=(i == 0), stop=True, skip_group_check=True)
                        pe.matmul(strided_pair(0, T, P), ident_r[:, :],
                                  neg_r[:, :].unsqueeze(1).to_broadcast([P, 2, P]),
                                  start=False, stop=True, skip_group_check=True)
                        pe.matmul(bank[:, 6, SEG[2]:SCORES], ident_r[:, :], neg_r[:, 0:TOK[2][1]],
                                  start=False, stop=True, skip_group_check=True).then_inc(z_done, 1)

            def layer(l):
                ffn(l, 0)
                mixer(l)
                ffn(l, 1)

            layers(pe, layer)
            sum_of_squares(3 * DEPTH, N_META, True)


def piece_stream(a):
    pieces = []

    def k_halves(w, c0, cols, halves=2):
        for half in range(halves):
            part = w[half * 4 * P:(half + 1) * 4 * P, c0:c0 + cols]
            pieces.append(part.reshape(4, P, cols).transpose(1, 0, 2).reshape(P, PIECE))

    def ffn(gu, down):
        for it in range(ITERS):
            k_halves(gu, it * 2 * P, 2 * P)
            k_halves(gu, D_FF + it * 2 * P, 2 * P)
        for q in range(QUADS):
            for c in range(ITERS - 2):
                part = down[c * 2 * P:(c + 1) * 2 * P, q * 4 * P:(q + 1) * 4 * P]
                pieces.append(part.reshape(2, P, 4, P).transpose(1, 2, 0, 3).reshape(P, PIECE))
            for half in range(2):
                part = down[(FC - 4) * P:, (q * 4 + half * 2) * P:(q * 4 + half * 2 + 2) * P]
                pieces.append(part.reshape(4, P, 2 * P).transpose(1, 0, 2).reshape(P, PIECE))

    for l in range(DEPTH):
        ffn(a["ffn1_w_gu"][l], a["ffn1_w_down"][l])
        for u in range(U_Y):
            k_halves(a["w_in"][l], u * 2 * P, 2 * P)
        for kind, pr in Y_UNITS:
            if kind == "r":
                k_halves(a["w_ret_proj"][l], pr * 2 * P, 2 * P)
            else:
                k_halves(a["w_sb_proj"][l], pr * 2 * P, 2 * P, halves=1)
        for u in range(PAIRS):
            k_halves(a["w_out"][l], u * 2 * P, 2 * P)
        ffn(a["ffn2_w_gu"][l], a["ffn2_w_down"][l])
    return np.stack(pieces)


def constants():
    f = np.float32
    row = np.arange(P)
    freq = f(10000.0) ** (-np.arange(0, DK, 2, dtype=f) / f(DK))
    angle = (np.arange(T, dtype=f)[None, :] * freq[row % 32][:, None]).astype(f)
    sign = np.where(row % DK < DK // 2, -1.0, 1.0)[:, None]
    tables = [np.cos(angle), sign * np.sin(angle)]
    for hd in range(HEADS):
        log_gamma = np.log(1.0 - 2.0 ** (-5.0 - hd))
        for t0, _ in TOK:
            diff = np.arange(T - t0)[None, :] - row[:, None]
            tables.append(np.where(diff >= 0, np.exp(log_gamma * np.maximum(diff, 0)), 0.0) * DK ** -0.5)
    key, query = row[:, None], row[None, :]
    squares = [np.full((P, P), 1.0 / P), np.eye(P), np.where(key >= query, NEG, 0.0),
               np.where(key >= query, -1.0, 0.0), np.full((P, P), -1.0)]
    return [np.ascontiguousarray(np.concatenate(x, axis=1), dtype=f) for x in (tables, squares)]


def kernel(**inputs):
    import concourse.bacc as bacc
    from concourse.bass_utils import run_bass_kernel_spmd

    a = {k: np.asarray(v) for k, v in inputs.items()}
    tokens = np.concatenate([a["meta"], a["x"][0]], axis=0)
    norms = [n for l in range(DEPTH) for n in (a["ffn1_norm"][l], a["mix_norm"][l], a["ffn2_norm"][l])]
    gains = np.stack(norms + [a["final_norm"]])
    arrays = {
        "stream": np.ascontiguousarray(piece_stream(a)),
        "tokens": np.ascontiguousarray(tokens.T.reshape(DC, P, T).transpose(1, 0, 2)),
        "gains": np.ascontiguousarray(gains.reshape(3 * DEPTH + 1, DC, P).transpose(2, 0, 1)),
        "gn_gains": np.ascontiguousarray(a["ret_gn"].reshape(DEPTH, HEADS, P).transpose(2, 0, 1)),
    }
    arrays["tables"], arrays["squares"] = constants()
    nc = bacc.Bacc("TRN2", target_bir_lowering=False, num_devices=1)
    args = [nc.dram_tensor(name, v.shape, mybir.dt.from_np(v.dtype), kind="ExternalInput").ap()
            for name, v in arrays.items()]
    out = nc.dram_tensor("out", (P, DC, SEQ), F32, kind="ExternalOutput").ap()
    trunk(nc, *args, out)
    got = run_bass_kernel_spmd(nc, [arrays], core_ids=[0]).results[0]["out"]
    return np.ascontiguousarray(got.transpose(2, 1, 0)).reshape(1, SEQ, D)
```
